# Optimizing a Trainium2 kernel written in Bass

```python
import math
import jax, jax.numpy as jnp
from jax import lax
import numpy as np

D_MODEL = 1024
BATCH = 1
SEQ = 1024
DEPTH = 2
DEC_BATCH = 1
DEC_SEQ = 64
PAST_LEN = 512

CHUNK = 64
WIDTH_A = 512
WIDTH_B = 512
MIX_WIDTH = WIDTH_A + WIDTH_B
SSM_GROUP_CH = 16
SSM_GROUPS = WIDTH_A // SSM_GROUP_CH
SSM_STATE = 64
POOL_WINDOWS = (2, 4, 8, 16)
POOL_GROUPS = len(POOL_WINDOWS)
POOL_GROUP_CH = WIDTH_B // POOL_GROUPS
POOL_HIST = max(POOL_WINDOWS) - 1
D_FF = 4 * D_MODEL
RMS_EPS = 1e-5
DT_MIN = 1e-3
DT_MAX = 1e-1

kernel_name = "s5_pool_hybrid_stream_step"

def rmsnorm(x, g):
    xf = x.astype(jnp.float32)
    y = xf * lax.rsqrt(jnp.mean(xf * xf, axis=-1, keepdims=True) + RMS_EPS)
    return (y * g.astype(jnp.float32)).astype(x.dtype)

def _scan_op(e1, e2):
    a1, b1 = e1
    a2, b2 = e2
    return a1 * a2, a2 * b1 + b2

def s5_mixer(u, h0, lam_re, lam_im, log_dt, b_re, b_im, c_re, c_im, d, w_glu):
    bsz, L, _ = u.shape
    f32 = jnp.float32
    lam = lax.complex(lam_re.astype(f32), lam_im.astype(f32))
    dt = jnp.exp(log_dt.astype(f32))[:, None]
    lam_dt = lam * dt
    lam_bar = jnp.exp(lam_dt)
    b = lax.complex(b_re.astype(f32), b_im.astype(f32))
    b_bar = ((lam_bar - 1.0) / lam)[..., None] * b
    c = lax.complex(c_re.astype(f32), c_im.astype(f32))
    blk = min(L, CHUNK)
    nblk = L // blk
    ug = u.astype(f32).reshape(bsz, nblk, blk, SSM_GROUPS, SSM_GROUP_CH).transpose(1, 0, 2, 3, 4)
    lam_pow = jnp.exp(lam_dt[None] * jnp.arange(1, blk + 1, dtype=f32)[:, None, None])
    a_elems = jnp.broadcast_to(lam_bar, (bsz, blk, SSM_GROUPS, SSM_STATE))

    def step(h, u_blk):
        bu = jnp.einsum('btgc,gpc->btgp', u_blk.astype(jnp.complex64), b_bar)
        _, hs = lax.associative_scan(_scan_op, (a_elems, bu), axis=1)
        hs = hs + lam_pow[None] * h[:, None]
        y = jnp.einsum('gcp,btgp->btgc', c, hs).real
        return hs[:, -1], y

    h_last, ys = lax.scan(step, h0, ug)
    y = ys.transpose(1, 0, 2, 3, 4).reshape(bsz, L, WIDTH_A)
    y = y + d.astype(f32) * u.astype(f32)
    z = jax.nn.gelu(y)
    out = z * jax.nn.sigmoid(z @ w_glu.astype(f32))
    return out.astype(u.dtype), h_last

def pool_mixer(u, hist, start_pos, w_pool, scale):
    bsz, L, _ = u.shape
    full = jnp.concatenate([hist.astype(u.dtype), u], axis=1)
    ff = full.astype(jnp.float32)
    cs0 = jnp.concatenate([jnp.zeros((bsz, 1, WIDTH_B), jnp.float32), lax.cumsum(ff, axis=1)], axis=1)
    pos = jnp.arange(L) + start_pos
    groups = []
    for k, w in enumerate(POOL_WINDOWS):
        sl = slice(k * POOL_GROUP_CH, (k + 1) * POOL_GROUP_CH)
        wsum = cs0[:, POOL_HIST + 1:POOL_HIST + 1 + L, sl] - cs0[:, POOL_HIST + 1 - w:POOL_HIST + 1 - w + L, sl]
        cnt = jnp.minimum(pos + 1, w).astype(jnp.float32)[None, :, None]
        groups.append(wsum / cnt)
    pooled = jnp.stack(groups, axis=2)
    diff = pooled - u.astype(jnp.float32).reshape(bsz, L, POOL_GROUPS, POOL_GROUP_CH)
    y = jnp.einsum('blkc,kcd->blkd', diff, w_pool.astype(jnp.float32)).reshape(bsz, L, WIDTH_B)
    y = y * scale.astype(jnp.float32)
    new_hist = full[:, -POOL_HIST:]
    return y.astype(u.dtype), new_hist

def trunk_layer(x, h0, pool_hist, start_pos, g_mix, g_ffn, w_in, lam_re, lam_im, log_dt,
                b_re, b_im, c_re, c_im, d, w_glu, w_pool, pool_scale, w_out, w_ff1, w_ff2):
    hn = rmsnorm(x, g_mix)
    proj = hn @ w_in
    u_a = proj[..., :WIDTH_A]
    u_b = proj[..., WIDTH_A:]
    y_a, h_last = s5_mixer(u_a, h0, lam_re, lam_im, log_dt, b_re, b_im, c_re, c_im, d, w_glu)
    y_b, new_hist = pool_mixer(u_b, pool_hist, start_pos, w_pool, pool_scale)
    x = x + jnp.concatenate([y_a, y_b], axis=-1) @ w_out
    hf = rmsnorm(x, g_ffn)
    x = x + jnp.square(jax.nn.relu(hf @ w_ff1)) @ w_ff2
    return x, h_last, new_hist

def setup_inputs(seed: int = 0) -> dict:
    key = jax.random.key(seed)
    ks = jax.random.split(key, 24)
    f32 = jnp.float32
    nrm = lambda k, s, sc: jax.random.normal(k, s, f32) * sc
    n_idx = jnp.arange(SSM_STATE, dtype=f32)
    lam_re = -0.5 + 0.01 * jax.random.normal(ks[5], (DEPTH, SSM_GROUPS, SSM_STATE), f32)
    lam_im = math.pi * n_idx[None, None, :] + 0.01 * jax.random.normal(ks[6], (DEPTH, SSM_GROUPS, SSM_STATE), f32)
    log_dt = jax.random.uniform(ks[7], (DEPTH, SSM_GROUPS), f32, math.log(DT_MIN), math.log(DT_MAX))
    return {
        "x_prompt": nrm(ks[0], (BATCH, SEQ, D_MODEL), 1.0),
        "x_sample": nrm(ks[1], (DEC_BATCH, DEC_SEQ, D_MODEL), 1.0),
        "state_ssm_re": nrm(ks[2], (DEPTH, DEC_BATCH, SSM_GROUPS, SSM_STATE), 0.1),
        "state_ssm_im": nrm(ks[3], (DEPTH, DEC_BATCH, SSM_GROUPS, SSM_STATE), 0.1),
        "state_pool": nrm(ks[4], (DEPTH, DEC_BATCH, POOL_HIST, WIDTH_B), 1.0),
        "g_mix": 1.0 + nrm(ks[8], (DEPTH, D_MODEL), 0.02),
        "g_ffn": 1.0 + nrm(ks[9], (DEPTH, D_MODEL), 0.02),
        "w_in": nrm(ks[10], (DEPTH, D_MODEL, MIX_WIDTH), D_MODEL ** -0.5),
        "ssm_lambda_re": lam_re,
        "ssm_lambda_im": lam_im,
        "ssm_log_dt": log_dt,
        "ssm_b_re": nrm(ks[11], (DEPTH, SSM_GROUPS, SSM_STATE, SSM_GROUP_CH), (2 * SSM_GROUP_CH) ** -0.5),
        "ssm_b_im": nrm(ks[12], (DEPTH, SSM_GROUPS, SSM_STATE, SSM_GROUP_CH), (2 * SSM_GROUP_CH) ** -0.5),
        "ssm_c_re": nrm(ks[13], (DEPTH, SSM_GROUPS, SSM_GROUP_CH, SSM_STATE), (2 * SSM_STATE) ** -0.5),
        "ssm_c_im": nrm(ks[14], (DEPTH, SSM_GROUPS, SSM_GROUP_CH, SSM_STATE), (2 * SSM_STATE) ** -0.5),
        "ssm_d": nrm(ks[15], (DEPTH, WIDTH_A), 1.0),
        "w_glu": nrm(ks[16], (DEPTH, WIDTH_A, WIDTH_A), WIDTH_A ** -0.5),
        "w_pool": nrm(ks[17], (DEPTH, POOL_GROUPS, POOL_GROUP_CH, POOL_GROUP_CH), POOL_GROUP_CH ** -0.5),
        "pool_scale": 1.0 + nrm(ks[18], (DEPTH, WIDTH_B), 0.05),
        "w_out": nrm(ks[19], (DEPTH, MIX_WIDTH, D_MODEL), MIX_WIDTH ** -0.5),
        "w_ff1": nrm(ks[20], (DEPTH, D_MODEL, D_FF), D_MODEL ** -0.5),
        "w_ff2": nrm(ks[21], (DEPTH, D_FF, D_MODEL), D_FF ** -0.5),
        "g_final": 1.0 + nrm(ks[22], (D_MODEL,), 0.02),
    }

def reference(x_prompt, x_sample, state_ssm_re, state_ssm_im, state_pool, g_mix, g_ffn, w_in,
              ssm_lambda_re, ssm_lambda_im, ssm_log_dt, ssm_b_re, ssm_b_im, ssm_c_re, ssm_c_im,
              ssm_d, w_glu, w_pool, pool_scale, w_out, w_ff1, w_ff2, g_final):
    f32 = jnp.float32
    xp = x_prompt
    xs = x_sample
    p_re, p_im, p_pool, s_re, s_im, s_pool = [], [], [], [], [], []
    for l in range(DEPTH):
        lw = (g_mix[l], g_ffn[l], w_in[l], ssm_lambda_re[l], ssm_lambda_im[l], ssm_log_dt[l],
              ssm_b_re[l], ssm_b_im[l], ssm_c_re[l], ssm_c_im[l], ssm_d[l], w_glu[l], w_pool[l],
              pool_scale[l], w_out[l], w_ff1[l], w_ff2[l])
        h0_p = jnp.zeros((xp.shape[0], SSM_GROUPS, SSM_STATE), jnp.complex64)
        hist_p = jnp.zeros((xp.shape[0], POOL_HIST, WIDTH_B), xp.dtype)
        xp, hp_last, hist_p_new = trunk_layer(xp, h0_p, hist_p, 0, *lw)
        p_re.append(hp_last.real)
        p_im.append(hp_last.imag)
        p_pool.append(hist_p_new)
        h0_s = lax.complex(state_ssm_re[l].astype(f32), state_ssm_im[l].astype(f32))
        xs, hs_last, hist_s_new = trunk_layer(xs, h0_s, state_pool[l], PAST_LEN, *lw)
        s_re.append(hs_last.real)
        s_im.append(hs_last.imag)
        s_pool.append(hist_s_new)
    y_prompt = rmsnorm(xp, g_final)
    y_sample = rmsnorm(xs, g_final)
    new_p_ssm_re = jnp.stack(p_re, axis=0)
    new_p_ssm_im = jnp.stack(p_im, axis=0)
    new_p_pool = jnp.stack(p_pool, axis=0)
    new_s_ssm_re = jnp.stack(s_re, axis=0)
    new_s_ssm_im = jnp.stack(s_im, axis=0)
    new_s_pool = jnp.stack(s_pool, axis=0)
    return (y_prompt, y_sample, new_p_ssm_re, new_p_ssm_im, new_p_pool, new_s_ssm_re, new_s_ssm_im, new_s_pool)


_drawn_inputs = setup_inputs


def setup_inputs(seed=0):
    import zlib

    import numpy as np

    out = dict(_drawn_inputs(seed))
    spreads = {}
    factors = {'ssm_lambda_re': 3.14, 'ssm_c_re': 3.127, 'ssm_c_im': 3.169, 'g_final': 2.815}
    for name, (base, spread) in spreads.items():
        noise = np.random.default_rng([zlib.crc32(name.encode()), seed]).standard_normal(out[name].shape)
        drawn = base * np.exp(spread * noise) if base else spread * noise
        out[name] = __import__('jax').numpy.asarray(drawn.astype(out[name].dtype))
    for name, factor in factors.items():
        out[name] = (out[name] * factor).astype(out[name].dtype)
    return out
```

```python
from contextlib import ExitStack

import numpy as np

import concourse.bass as bass
from concourse import mybir

F32 = mybir.dt.float32
F32R = mybir.dt.float32r
ALU = mybir.AluOpType
ACT = mybir.ActivationFunctionType

P = 128
DM = 1024
LAYERS = 2
SEQ, DSEQ = 1024, 64
BLK = 8
JP, JS = SEQ // BLK, DSEQ // BLK
J = JP + JS
T = BLK * J
KD = DM // P
KA = 4
DFF = 4 * DM
GROUPS, CH, ST = 32, 16, 64
GP = GROUPS // 2
EPS = 1e-5
CHUNKS = ((0, 3), (3, 6), (6, 8))
WIDE = 3 * J

B_WIN, B_WOB, B_GLU, B_WOA, B_FF = 0, 8, 12, 14, 18
FFC = DFF // P // KD
NB = B_FF + 2 * KD * FFC
T_WIN, T_POOL, T_WOB, T_GLU, T_WOA, T_FF = 0, 8, 12, 20, 24, 32
NT = T_FF + 2 * KD * FFC
S_SUM1, S_PREP, S_DRIVE, S_SUM2 = 0, 3, 19, 35
NS = 38

NM = 17
C_LRE, C_LIM, C_LDT = 0, 16, 32
C_M = 48
C_BRE = C_M + NM * GP
C_BIM, C_CRE, C_CIM = C_BRE + 256, C_BRE + 512, C_BRE + 768
C_ID = C_BRE + 1024
C_HIST = C_ID + 128
C_RC = C_HIST + 64
NPP = C_RC + 64

L_FFN, L_NEXT, L_SCALE, NLP = 0, 8, 16, 20
D_D, D_INIT, ND = 0, 32, 64

TWO_PI = 6.283185307179586
C1 = 6.28125
C2 = 0.00193500518798828125
C3 = TWO_PI - C1 - C2
MAGIC = 12582912.0


def hybrid_trunk(nc, x_in, w_blocks, w_pool, prep_in, gain0, layer_in, dstate_in,
                 y_out, pool_out, ssm_out):
    x_hist = nc.dram_tensor("x_kept", (LAYERS + 1, KD, P, T), F32, kind="Internal").ap()
    ua_dram = nc.dram_tensor("ua_dram", (KA * P, BLK, J), F32, kind="Internal").ap()
    ya_dram = nc.dram_tensor("ya_dram", (KA * P, BLK, J), F32, kind="Internal").ap()
    bt_dram = nc.dram_tensor("bt_dram", (P, GP, 2, P), F32, kind="Internal").ap()
    cy_dram = nc.dram_tensor("cy_dram", (P, GP, 2, P), F32, kind="Internal").ap()
    k_dram = nc.dram_tensor("k_dram", (CH, GROUPS, 240), F32, kind="Internal").ap()

    with ExitStack() as ctx:
        base = ((nc.sbuf_base + 31) // 32) * 32
        words = (nc.sbuf_usable_end - base) // 4

        def at(name, offset, shape, dt=F32):
            assert offset + int(np.prod(shape[1:])) <= words, name
            return nc.alloc_sbuf_tensor_at(name, list(shape), dt, offset=base + 4 * offset)

        def sem(name):
            return ctx.enter_context(nc.semaphore(name))

        x = at("x", 0, [P, KD, T])
        ub = at("ub", 0, [P, KA, BLK, J + 4])
        s0 = at("pool_s0", 4480, [P, BLK, J + 4])
        s1 = at("pool_s1", 5600, [P, BLK, J + 4])
        H = KD * T
        hhi = at("h_high", H, [P, KD, T], F32R)
        hlo = at("h_low", 2 * H, [P, KD, T], F32R)
        bt = at("drive_weights", H, [P, GP, 2, P])
        zh = at("states", H, [P, GP, 2, J])
        cy = at("carry_weights", H + 4352, [P, GP, 2, P])
        kin = at("intra_weights", H + 8448, [P, GROUPS, P])
        dd = at("d_and_init", H + 12544, [P, ND])
        fin = at("final_states", H + 12544 + ND, [P, 2, 2, GP])
        rot = at("rotations", H + 13056, [P, 2, GP, JP])
        ya = at("y_a", H + 13056, [P, KA, T])
        zhi = at("z_high", H, [P, KA, T], F32R)
        zlo = at("z_low", H + 4352, [P, KA, T], F32R)
        G = 3 * H
        ghi = at("hidden_high", G, [P, KD, T], F32R)
        glo = at("hidden_low", G + 8704, [P, KD, T], F32R)
        ua = at("u_a", G, [P, KA, T])
        w = at("drive", G, [P, GP, 2, J])
        ublk = at("u_blocks", G + 4352, [P, GROUPS, J])
        yah = at("y_a_high", G, [P, KA, T], F32R)
        yal = at("y_a_low", G + 4352, [P, KA, T], F32R)
        ybh = at("y_b_high", G + 8704, [P, KA, T], F32R)
        ybl = at("y_b_low", G + 13056, [P, KA, T], F32R)
        o = G + 8704
        pp = at("prep_in", o, [P, NPP])
        o += NPP
        pwr = at("power_re", o, [P, NM, GP])
        pwi = at("power_im", o + 272, [P, NM, GP])
        bbr = at("bbar_re", o + 544, [P, GP, CH])
        bbi = at("bbar_im", o + 800, [P, GP, CH])
        nci = at("minus_c_im", o + 1056, [P, GP, CH])
        o += 1312
        pa_mag = at("prep_mag", o, [P, NM, GP])
        pa_th = at("prep_phase", o + 272, [P, NM, GP])
        pa_k = at("prep_turns", o + 544, [P, NM, GP])
        pa_r = at("prep_reduced", o + 816, [P, NM, GP])
        pa_s = at("prep_sine", o + 1088, [P, NM, GP])
        pa_q = at("prep_small", o + 1360, [P, 12, GP])
        btst = at("bt_stage", o, [P, 4, 2, P])
        o += 1632
        xq = at("x_quarter", o, [P, 2, 4, BLK, CH])
        yq = at("y_quarter", o + 1024, [P, 2, 4, BLK + 1, CH])
        pt = at("prep_products", o + 2176, [P, 2, 576])
        kst = at("k_stage", o + 3328, [CH, 4, P])
        R = G + 2 * H
        raw = at("w_raw", R, [P, 2, 1024])
        whi = at("w_high", R + 2048, [P, 2, 1024], F32R)
        wlo = at("w_low", R + 4096, [P, 2, 1024], F32R)
        A = R + 6144
        rms = at("rms", A, [P, T])
        tr = at("work_r", A + 1088, [P, T])
        ts = at("work_s", A + 2176, [P, T])
        dtmp = at("dve_products", A, [P, 2, 512])
        ptmp = at("pool_products", A + 1024, [P, 2, 512])
        hist = at("hist_out", A + 1088, [P, KA, BLK, 2, 2])
        zero = at("zeros", G + 8704 + NPP + 1312 + 1632, [CH, 112])
        wp = at("w_pool_sb", A + 1088 + 128, [P, KA, P])
        S = A + 3264
        ones = at("ones", S, [P, P])
        g0 = at("gain_0", S + 128, [P, KD])
        lp = at("layer_params", S + 136, [P, NLP])
        rmag = at("decay", S + 160, [P, GP])
        phase = at("phasor", S + 176, [P, 2, GP])
        eps_col = at("epsilon", S + 208, [P, 1])

        ps = [ctx.enter_context(nc.psum_tensor(f"tile{i}", [P, 3, 512], F32)) for i in range(2)]
        sm = [ctx.enter_context(nc.psum_tensor(f"small{i}", [P, 512], F32)) for i in range(2)]

        raw_landed = [sem(f"raw_landed{i}") for i in range(2)]
        whi_made = sem("whi_made")
        wlo_made = sem("wlo_made")
        tile_done = sem("tile_done")
        tile_free = sem("tile_free")
        small_done = sem("small_done")
        small_free = sem("small_free")
        carry_done = sem("carry_done")
        carry_free = sem("carry_free")
        const_in = sem("const_in")
        x_in_s = [sem(f"x_in{i}") for i in range(KD)]
        sq_made = sem("sq_made")
        sq_added = sem("sq_added")
        hhi_made = sem("hhi_made")
        h_made = sem("h_made")
        x_kept = sem("x_kept_s")
        rstd = sem("rstd")
        ones_set = sem("ones_set")
        dve = sem("dve_step")
        pool_s = sem("pool_step")
        pp_in = sem("pp_in")
        lp_in = sem("lp_in")
        prep_v = sem("prep_v")
        prep_a = sem("prep_a")
        pe_passed = sem("pe_passed")
        pool_passed = sem("pool_passed")
        x_quart = sem("x_quart")
        y_quart = sem("y_quart")
        bt_out = sem("bt_out")
        cy_out = sem("cy_out")
        k_out = sem("k_out")
        zero_set = sem("zero_set")
        k_zero = sem("k_zero")
        ua_out = sem("ua_out")
        ublk_in = sem("ublk_in")
        hist_made = sem("hist_made")
        hist_out_s = sem("hist_out_s")
        diff_made = sem("diff_made")
        wp_in = sem("wp_in")
        ybh_made = sem("ybh_made")
        x_back = [sem(f"x_back{i}") for i in range(KD)]
        bt_in = sem("bt_in")
        cy_in = sem("cy_in")
        kin_in = sem("kin_in")
        dd_in = sem("dd_in")
        rot_made = sem("rot_made")
        pre_p = sem("pre_p")
        scan_v = sem("scan_v")
        st_v = sem("st_v")
        st_p = sem("st_p")
        fin_made = sem("fin_made")
        fin_out = sem("fin_out")
        ya_out = [sem(f"ya_out{i}") for i in range(4)]
        ya_in = [sem(f"ya_in{i}") for i in range(4)]
        gelu_made = sem("gelu_made")
        z_made = sem("z_made")
        zlo_made = sem("zlo_made")
        sig_made = sem("sig_made")
        yah_made = sem("yah_made")
        ya_made = sem("ya_made")
        sq_v = sem("sq_v")
        ghi_made = sem("ghi_made")
        hid_made = sem("hid_made")
        y_made = sem("y_made")
        y_out_s = sem("y_out_s")

        def tile_of(t, m):
            return t[:, bass.ds(m, 1), :].rearrange("p a n -> p (a n)")

        def f32(ap):
            return ap.bitcast(F32)

        def halves(tile, flat, also=()):
            yield (tile[:, 0:2, 0:WIDE], flat[:, 0:2 * WIDE].rearrange("p (c n) -> p c n", c=2),
                   *(a[:, 0:2 * WIDE].rearrange("p (c n) -> p c n", c=2) for a in also))
            yield (tile[:, 2, 0:2 * J], flat[:, 2 * WIDE:T], *(a[:, 2 * WIDE:T] for a in also))

        class Steps:

            def __init__(self, eng, semaphore):
                self.eng, self.sem, self.base, self.n = eng, semaphore, 0, 0

            def __call__(self, ins):
                ins.then_inc(self.sem, 1)
                self.n += 1

            def wait(self):
                if self.n:
                    self.eng.wait_ge(self.sem, self.base + self.n)

            def enter(self, i, per_turn):
                self.saved = (self.base, self.n)
                self.base, self.n = self.base + self.n + i * per_turn, 0

            def leave(self, turns, per_turn):
                assert self.n == per_turn, (self.n, per_turn)
                self.base, self.n = self.saved[0], self.saved[1] + turns * per_turn

        def quarter(t, q, *rest):
            return t[(slice(None), slice(4 * q, 4 * q + 4), *rest)]

        def rotate(step, tensor_tensor, tmp, q, src, dst, shift, sign, told=None):
            for a, n in ((0, JP - shift), (JP, JS - shift)):
                cos, sin = (quarter(rot[:, i], q, slice(0, n)) for i in range(2))
                re, im = (quarter(src, q, i, slice(a, a + n)) for i in range(2))
                t0, t1 = (tmp[:, i, 0:4 * n].rearrange("p (g j) -> p g j", j=n) for i in range(2))
                for ri, (u, w_, op) in enumerate(((re, im, ALU.subtract if sign > 0 else ALU.add),
                                                  (im, re, ALU.add if sign > 0 else ALU.subtract))):
                    step.wait()
                    step(tensor_tensor(t0, cos, u, ALU.mult))
                    step(tensor_tensor(t1, sin, w_, ALU.mult))
                    step.wait()
                    ins = tensor_tensor(quarter(dst, q, ri, slice(a + shift, a + shift + n)), t0, t1, op)
                    if told is not None and a and ri:
                        ins.then_inc(told, 1)
                    else:
                        step(ins)

        block = ctx.enter_context(nc.Block())

        @block.sync
        def _(sp):
            sp.dma_start(g0[:, :], gain0).then_inc(const_in, 16)
            for s in range(2):
                sp.dma_start(raw[:, s, :], w_blocks[s]).then_inc(raw_landed[s], 16)
            with sp.Fori(1, LAYERS * NB // 2 + 1) as i:
                for s in range(2):
                    b = 2 * i + s
                    sp.wait_ge(wlo_made, b - 1)
                    sp.dma_start(raw[:, s, :], w_blocks[bass.ds(b, 1)].rearrange("a p n -> (a p) n")).then_inc(raw_landed[s], 16)
            sp.wait_ge(raw_landed[0], 16 * (LAYERS * NB // 2 + 1))
            sp.wait_ge(raw_landed[1], 16 * (LAYERS * NB // 2 + 1))

        @block.tensor
        def _(pe):
            def product(tile, slot, half, n_k, xh, xl, ready=None):
                for k in range(n_k):
                    if ready:
                        ready(k)
                    for n, (wt, xt) in enumerate(((whi, xh), (whi, xl), (wlo, xh))):
                        lhs = wt[:, slot, (half * n_k + k) * P:(half * n_k + k + 1) * P]
                        for c, (a, b) in enumerate(CHUNKS):
                            last = pe.matmul(ps[tile][:, c, 0:(b - a) * J], lhs, xt[:, k, a * J:b * J],
                                             start=(k == 0 and n == 0), stop=(k == n_k - 1 and n == 2))
                last.then_inc(tile_done, 1)

            def tile_at(n):
                pe.wait_ge(tile_free, n + 1)

            def block_at(b):
                pe.wait_ge(wlo_made, b + 1)

            def small_at(n):
                pe.wait_ge(small_free, n + 1)

            def sum_part(s, c, first, phase_no):
                a, b = CHUNKS[c]
                small_at(first + s + c)
                pe.wait_ge(sq_added, 7 * phase_no + 7)
                pe.matmul(sm[(s + c) % 2][:, 0:(b - a) * J], ones[:, :], rms[:, a * J:b * J],
                          start=True, stop=True).then_inc(small_done, 1)

            pe.wait_ge(ones_set, 1)
            with pe.Fori(0, LAYERS) as l:
                LB, LT, LS = l * NB, l * NT, l * NS

                def prep(q):
                    s = S_PREP + 4 * q
                    pe.wait_ge(x_quart, l * 4 + q + 1)
                    for ri in range(2):
                        small_at(LS + s + ri)
                        for g in range(4):
                            mm = pe.transpose(sm[(s + ri) % 2][:, g * P:(g + 1) * P],
                                              xq[:, ri, g, :, :].rearrange("p t c -> p (t c)"),
                                              pp[:, C_ID:C_ID + P])
                        mm.then_inc(small_done, 1)
                    pe.wait_ge(y_quart, l * 4 + q + 1)
                    for gl in range(2):
                        small_at(LS + s + 2 + gl)
                        pe.sem_inc(pe_passed, 1)
                        rows = slice(ST * gl, ST * gl + ST)
                        for g in range(4):
                            for ri, b in enumerate((bbr, bbi)):
                                mm = pe.matmul(sm[(s + gl) % 2][0:CH, g * P:(g + 1) * P], b[rows, 4 * q + g, :],
                                               yq[rows, ri, g, 0:BLK, :].rearrange("p t c -> p (t c)"),
                                               start=(ri == 0), stop=(ri == 1))
                        mm.then_inc(small_done, 1)

                for t in range(KD):
                    tile_at(LT + t)
                    block_at(LB + t)

                    def ready(k):
                        if t == 0:
                            pe.wait_ge(h_made, l * 16 + k + 1)
                        if t == 1 and k == 2:
                            sum_part(S_SUM1, 2, LS, 2 * l)
                    product(t % 2, t % 2, 0, KD, hhi, hlo, ready)
                    if t == 0:
                        sum_part(S_SUM1, 0, LS, 2 * l)
                        sum_part(S_SUM1, 1, LS, 2 * l)
                    q = {2: 0, 3: 1, 5: 2, 7: 3}.get(t)
                    if q is not None:
                        prep(q)
                pe.wait_ge(wp_in, 16 * (l + 1))
                for i in range(KA):
                    k = KA - 1 - i
                    tile_at(LT + T_POOL + i)
                    pe.wait_ge(diff_made, l * KA + i + 1)
                    for c, (a, b) in enumerate(CHUNKS):
                        out = ps[i % 2][:, c, 0:(b - a) * J].rearrange("p (t j) -> p t j", j=J)
                        pe.matmul(out[:, :, 0:JP], wp[:, k, :], ub[:, k, a:b, 2:2 + JP], start=True, stop=True)
                        mm = pe.matmul(out[:, :, JP:J], wp[:, k, :], ub[:, k, a:b, JP + 4:J + 4],
                                       start=True, stop=True)
                    mm.then_inc(tile_done, 1)

                def half_blocks(b0, t0, i, xh, xl, ready):
                    block_at(LB + b0 + i)
                    for h in range(2):
                        tile_at(LT + t0 + 2 * i + h)
                        product(h, i % 2, h, KA, xh, xl, ready if i == 0 and h == 0 else None)

                for i in range(4):
                    half_blocks(B_WOB, T_WOB, i, ybh, ybl,
                                lambda k: pe.wait_ge(tile_free, LT + T_POOL + KA + 2))
                    if i == 0:
                        pe.wait_ge(bt_in, 16 * (l + 1))
                        pe.wait_ge(ublk_in, 16 * BLK * (l + 1))
                        for g in range(GP):
                            n = S_DRIVE + g
                            small_at(LS + n)
                            for gl in range(2):
                                for ri in range(2):
                                    mm = pe.matmul(sm[n % 2][ST * gl:ST * gl + ST, ri * J:(ri + 1) * J],
                                                   bt[:, g, ri, ST * gl:ST * gl + ST], ublk[:, 2 * g + gl, :],
                                                   start=True, stop=True)
                            mm.then_inc(small_done, 1)
                pe.wait_ge(small_free, LS + S_SUM2 + 2)
                pe.wait_ge(kin_in, 16 * BLK * (l + 1))
                pe.wait_ge(cy_in, 16 * (l + 1))
                for u in range(GP):
                    if u >= 2:
                        pe.wait_ge(carry_free, l * GP + u - 1)
                    if u in (0, 4):
                        pe.wait_ge(st_v, l * 2 + u // 4 + 1)
                    if u in (8, 12):
                        pe.wait_ge(st_p, l * 2 + u // 4 - 1)
                    gl = u % 2
                    rows = slice(ST * gl, ST * gl + ST)
                    for i in range(2):
                        g = u - gl + i
                        out = sm[gl][:, i * J:(i + 1) * J]
                        pe.matmul(out, kin[:, 2 * g + gl, :], ublk[:, 2 * g + gl, :], start=True, stop=False)
                        pe.matmul(out, cy[rows, g, 0, :], zh[rows, g, 0, :], start=False, stop=False)
                        mm = pe.matmul(out, cy[rows, g, 1, :], zh[rows, g, 1, :], start=False, stop=True)
                    mm.then_inc(carry_done, 1)
                for i in range(2):
                    half_blocks(B_GLU, T_GLU, i, zhi, zlo, lambda k: pe.wait_ge(zlo_made, l * KA + k + 1))
                for i in range(4):
                    half_blocks(B_WOA, T_WOA, i, yah, yal, lambda k: pe.wait_ge(ya_made, l * KA + k + 1))

                def ff_tile(slot, n, xh, xl, ready=None):
                    tile_at(LT + T_FF + n)
                    block_at(LB + B_FF + n)
                    product(slot, slot, 0, KD, xh, xl, ready)

                def ff2(c, m, odd):
                    ff_tile(odd, 16 * c + 8 + m, ghi, glo,
                            None if odd else lambda k: pe.wait_ge(hid_made, l * 32 + 8 * c + k + 1))

                pe.wait_ge(carry_free, l * GP + GP)
                for m in range(KD):
                    def ready(k):
                        if m == 0:
                            pe.wait_ge(h_made, l * 16 + 8 + k + 1)
                        if m == 1 and k == 2:
                            sum_part(S_SUM2, 2, LS, 2 * l + 1)
                    ff_tile(m % 2, m, hhi, hlo, ready)
                    if m == 0:
                        sum_part(S_SUM2, 0, LS, 2 * l + 1)
                        sum_part(S_SUM2, 1, LS, 2 * l + 1)
                with pe.Fori(0, FFC - 1) as c:
                    with pe.Fori(0, KD // 2) as m2:
                        for odd in range(2):
                            ff2(c, 2 * m2 + odd, odd)
                    with pe.Fori(0, KD // 2) as m2:
                        for odd in range(2):
                            ff_tile(odd, 16 * c + 16 + 2 * m2 + odd, hhi, hlo)
                for m in range(KD):
                    ff2(FFC - 1, m, m % 2)
            for c in range(3):
                sum_part(S_SUM1, c, LAYERS * NS, 2 * LAYERS)

        @block.scalar
        def _(act):
            act.sem_inc(small_free, 2)

            def split_hi(b, s):
                act.wait_ge(raw_landed[s], 16 * (b + 1))
                act.activation(whi[:, s, :], raw[:, s, :], ACT.Copy).then_inc(whi_made, 1)

            def finish(m, phase_no, gain, keep):
                if m > 2:
                    act.wait_ge(sq_added, 7 * phase_no + m - 2)
                dst = (tr, ts)[m % 2] if m else rms
                act.activation(dst[:, :], x[:, m, :], ACT.Square).then_inc(sq_made, 1)
                act.activation(hhi[:, m, :], x[:, m, :], ACT.Copy, scale=gain[:, m:m + 1]).then_inc(hhi_made, 1)
                if keep is not None:
                    act.dma_start(keep, x[:, m, :]).then_inc(x_kept, 16)

            def roots(s, first):
                for c, (a, b) in enumerate(CHUNKS):
                    act.wait_ge(small_done, first + s + c + 1)
                    act.activation(rms[:, a * J:b * J], sm[(s + c) % 2][:, 0:(b - a) * J], ACT.Sqrt,
                                   scale=1.0 / DM, bias=eps_col[:, :]).then_inc(small_free, 1)

            for m in range(KD):
                act.dma_start(x[:, m, :], x_in[m]).then_inc(x_in_s[m], 16)
            split_hi(0, 0)
            act.wait_ge(const_in, 16)
            for m in range(KD):
                act.wait_ge(x_in_s[m], 16)
                finish(m, 0, g0, x_hist[0, m])
            split_hi(0, 1)
            act.wait_ge(ones_set, 1)

            with act.Fori(0, LAYERS) as l:
                LB, LT, LS = l * NB, l * NT, l * NS

                def ahead(b, t):
                    act.wait_ge(tile_done, LT + t + 1)
                    split_hi(l * (NB // 2) + b // 2 + 1, b % 2)

                def prep(q):
                    s = S_PREP + 4 * q
                    for ri in range(2):
                        act.wait_ge(small_done, LS + s + ri + 1)
                        if ri == 0 and q:
                            act.wait_ge(bt_out, 16 * (l * 4 + q))
                        act.activation(btst[:, :, ri, :], sm[(s + ri) % 2][:, :].rearrange("p (g n) -> p g n", n=P),
                                       ACT.Copy).then_inc(small_free, 1)
                    act.wait_ge(small_free, LS + s + 2 + 2)
                    act.dma_start(bt_dram[:, 4 * q:4 * q + 4, :, :], btst[:, :, :, :]).then_inc(bt_out, 16)
                    for hb in range(2):
                        act.wait_ge(small_done, LS + s + 2 + hb + 1)
                        if q or hb:
                            act.wait_ge(k_out, 16 * (l * 8 + 2 * q + hb))
                        act.activation(kst[:, :, :], sm[(s + hb) % 2][0:CH, :].rearrange("p (g n) -> p g n", n=P),
                                       ACT.Copy).then_inc(small_free, 1)
                        act.wait_ge(small_free, LS + s + 2 + hb + 1 + 2)
                        act.dma_start(k_dram[:, 8 * q + hb:8 * q + 8:2, 112:240], kst[:, :, :]).then_inc(k_out, 16)

                roots(S_SUM1, LS)
                ahead(0, 0)
                act.wait_ge(pp_in, 16 * (l + 1))
                act.activation(pa_q[:, 0, :], pp[:, C_LDT:C_LDT + GP], ACT.Exp).then_inc(prep_a, 1)
                act.wait_ge(prep_v, l * 2 + 1)
                act.activation(pa_mag[:, :, :], pa_mag[:, :, :], ACT.Exp).then_inc(prep_a, 1)
                act.activation(pa_s[:, :, :], pa_r[:, :, :], ACT.Sin).then_inc(prep_a, 1)
                act.activation(pa_k[:, :, :], pa_r[:, :, :], ACT.Sin, scale=0.5).then_inc(prep_a, 1)
                for t in range(1, KD):
                    ahead(t, t)
                    q = {2: 0, 3: 1, 5: 2, 7: 3}.get(t)
                    if q is not None:
                        prep(q)
                act.wait_ge(bt_out, 64 * (l + 1))
                act.wait_ge(k_out, 128 * (l + 1))
                act.wait_ge(cy_out, 128 * (l + 1))
                act.wait_ge(diff_made, l * KA + KA)
                act.wait_ge(lp_in, 16 * (l + 1))
                for i in range(KA):
                    k = KA - 1 - i
                    act.wait_ge(tile_done, LT + T_POOL + i + 1)
                    for pt_, out in halves(ps[i % 2], ybh[:, k, :]):
                        ins = act.activation(out, pt_, ACT.Copy, scale=lp[:, L_SCALE + k:L_SCALE + k + 1])
                    ins.then_inc(ybh_made, 1)
                ahead(B_WOB, T_WOB + 1)
                act.wait_ge(ua_out, 64 * (l + 1))
                for g in range(GP):
                    n = S_DRIVE + g
                    act.wait_ge(small_done, LS + n + 1)
                    act.activation(w[:, g, :, :], sm[n % 2][:, 0:2 * J].rearrange("p (r j) -> p r j", j=J),
                                   ACT.Copy).then_inc(small_free, 1)
                for i in range(1, 4):
                    ahead(B_WOB + i, T_WOB + 2 * i + 1)
                for q in range(4):
                    act.wait_ge(carry_free, l * GP + 4 * q + 4)
                    for tau in range(BLK):
                        act.dma_start(ya_dram[q * P:(q + 1) * P, tau, :].rearrange("(g c) j -> c g j", c=CH),
                                      ublk[CH * tau:CH * tau + CH, 8 * q:8 * q + 8, :]).then_inc(ya_out[q], 16)
                act.wait_ge(fin_made, 4 * (l + 1))
                for q in range(4):
                    act.wait_ge(ya_out[q], 16 * BLK * (l + 1))
                    act.dma_start(ya[:, q, :], ya_dram[q * P:(q + 1) * P].rearrange("a t j -> a (t j)")).then_inc(ya_in[q], 16)
                act.wait_ge(carry_done, l * GP + GP)
                for q in range(4):
                    act.wait_ge(ya_in[q], 16 * (l + 1))
                    act.activation(ya[:, q, :], ya[:, q, :], ACT.Gelu_apprx_tanh).then_inc(gelu_made, 1)
                    act.wait_ge(gelu_made, l * KA + q + 1)
                    act.activation(zhi[:, q, :], ya[:, q, :], ACT.Copy).then_inc(z_made, 1)
                act.wait_ge(fin_out, 16 * (l + 1))
                for m in range(KA):
                    act.wait_ge(tile_done, LT + T_GLU + m + 1)
                    for pt_, out in halves(ps[m % 2], (tr, ts)[m % 2][:, :]):
                        ins = act.activation(out, pt_, ACT.Sigmoid)
                    ins.then_inc(sig_made, 1)
                    if m % 2:
                        ahead(B_GLU + m // 2, T_GLU + m)
                    act.wait_ge(tile_free, LT + T_GLU + m + 1 + 2)
                    act.activation(yah[:, m, :], ya[:, m, :], ACT.Copy).then_inc(yah_made, 1)
                for m in range(KD):
                    act.wait_ge(tile_free, LT + T_WOA + m + 1 + 2)
                    finish(m, 2 * l + 1, lp[:, L_FFN:L_FFN + KD], None)
                    if m % 2:
                        ahead(B_WOA + m // 2, T_WOA + m)

                def hidden(n, c, out):
                    act.wait_ge(tile_free, LT + T_FF + 16 * c + n + 1 + 2)
                    act.activation(out, tr[:, :], ACT.Square).then_inc(ghi_made, 1)

                def ahead_ff(c, n, m2, odd):
                    act.wait_ge(tile_done, LT + T_FF + 16 * c + n + 2 * m2 + odd + 1)
                    split_hi(l * (NB // 2) + (B_FF + n) // 2 + 8 * c + m2 + 1, odd)

                roots(S_SUM2, LS)
                for m in range(KD):
                    hidden(m, 0, ghi[:, m, :])
                    ahead_ff(0, 0, m // 2, m % 2)
                with act.Fori(0, FFC - 1) as c:
                    with act.Fori(0, KD // 2) as m2:
                        for odd in range(2):
                            ahead_ff(c, 8, m2, odd)
                    with act.Fori(0, KD // 2) as m2:
                        for odd in range(2):
                            m = 2 * m2 + odd
                            hidden(m, c + 1, tile_of(ghi, m))
                            ahead_ff(c, 16, m2, odd)
                for m in range(KD):
                    act.wait_ge(tile_free, LT + T_FF + 16 * (FFC - 1) + 8 + m + 1 + 2)
                    finish(m, 2 * l + 2, lp[:, L_NEXT:L_NEXT + KD], x_hist[bass.ds(l + 1, 1), m].rearrange("a p n -> (a p) n"))
                    ahead_ff(FFC - 1, 8, m // 2, m % 2)

            roots(S_SUM1, LAYERS * NS)
            for m in range(KD):
                act.wait_ge(y_made, m + 1)
                act.dma_start(y_out[m], x[:, m, :]).then_inc(y_out_s, 16)
            act.wait_ge(y_out_s, 16 * KD)
            act.wait_ge(x_kept, 16 * KD * (LAYERS + 1))
            act.wait_ge(hist_out_s, 16 * LAYERS)
            act.wait_ge(fin_out, 16 * LAYERS)

        @block.vector
        def _(v):
            step = Steps(v, dve)
            v.sem_inc(tile_free, 2)

            def split_lo(b, s):
                v.wait_ge(whi_made, b + 1)
                v.tensor_tensor(wlo[:, s, :], raw[:, s, :], f32(whi[:, s, :]), ALU.subtract).then_inc(wlo_made, 1)

            def low_h(m, n, gain):
                v.wait_ge(hhi_made, n + 1)
                v.scalar_tensor_tensor(hlo[:, m, :], x[:, m, :], gain[:, m:m + 1], f32(hhi[:, m, :]),
                                       ALU.mult, ALU.subtract).then_inc(h_made, 1)

            def inverse(s, first, n):
                for c, (a, b) in enumerate(CHUNKS):
                    v.wait_ge(small_free, first + s + c + 1 + 2)
                    v.reciprocal(rms[:, a * J:b * J], rms[:, a * J:b * J]).then_inc(rstd, 1)
                v.wait_ge(rstd, n + 3)

            v.memset(eps_col[:, :], EPS)
            v.memset(ones[:, :], 1.0).then_inc(ones_set, 1)
            v.memset(zero[:, :], 0.0).then_inc(zero_set, 1)
            split_lo(0, 0)
            v.wait_ge(const_in, 16)
            for m in range(KD):
                v.wait_ge(x_in_s[m], 16)
                low_h(m, m, g0)
            split_lo(1, 1)

            with v.Fori(0, LAYERS) as l:
                LB, LT = l * NB, l * NT
                step.enter(l, DVE_STEPS)

                def ahead(b):
                    split_lo(LB + b + 2, b % 2)

                def tt(out, a, b, op):
                    step(v.tensor_tensor(out, a, b, op))

                def ttw(out, a, b, op):
                    step.wait()
                    tt(out, a, b, op)

                def over(ap, n):
                    return ap.unsqueeze(1).broadcast_to([P, n, GP])

                def prep():
                    lre, lim = pp[:, C_LRE:C_LRE + GP], pp[:, C_LIM:C_LIM + GP]
                    ms = pp[:, C_M:C_M + NM * GP].rearrange("p (m g) -> p m g", g=GP)
                    v.wait_ge(prep_a, l * 4 + 1)
                    tt(pa_q[:, 1, :], lre, pa_q[:, 0, :], ALU.mult)
                    tt(pa_q[:, 2, :], lim, pa_q[:, 0, :], ALU.mult)
                    step.wait()
                    tt(pa_mag[:, :, :], ms, over(pa_q[:, 1, :], NM), ALU.mult)
                    tt(pa_th[:, :, :], ms, over(pa_q[:, 2, :], NM), ALU.mult)
                    step.wait()
                    step(v.tensor_scalar(pa_k[:, :, :], pa_th[:, :, :], 1.0 / TWO_PI, MAGIC, ALU.mult, ALU.add))
                    step.wait()
                    step(v.tensor_scalar(pa_k[:, :, :], pa_k[:, :, :], MAGIC, None, ALU.subtract))
                    step.wait()
                    step(v.scalar_tensor_tensor(pa_r[:, :, :], pa_k[:, :, :], -C1, pa_th[:, :, :], ALU.mult, ALU.add))
                    step.wait()
                    step(v.scalar_tensor_tensor(pa_r[:, :, :], pa_k[:, :, :], -C2, pa_r[:, :, :], ALU.mult, ALU.add))
                    step.wait()
                    step(v.scalar_tensor_tensor(pa_r[:, :, :], pa_k[:, :, :], -C3, pa_r[:, :, :], ALU.mult, ALU.add))
                    step.wait()
                    v.tensor_scalar(pa_r[:, :, :], pa_r[:, :, :], 3.1415925, -3.1415925, ALU.min,
                                    ALU.max).then_inc(prep_v, 1)
                    v.wait_ge(prep_a, l * 4 + 4)
                    tt(pa_th[:, :, :], pa_k[:, :, :], pa_k[:, :, :], ALU.mult)
                    step.wait()
                    step(v.tensor_scalar(pa_th[:, :, :], pa_th[:, :, :], -2.0, 1.0, ALU.mult, ALU.add))
                    step.wait()
                    tt(pwr[:, :, :], pa_mag[:, :, :], pa_th[:, :, :], ALU.mult)
                    tt(pwi[:, :, :], pa_mag[:, :, :], pa_s[:, :, :], ALU.mult)
                    step(v.tensor_copy(rmag[:, :], pa_mag[:, NM - 1, :]))
                    step(v.tensor_copy(phase[:, 0, :], pa_th[:, NM - 1, :]))
                    step(v.tensor_copy(phase[:, 1, :], pa_s[:, NM - 1, :]))
                    step.wait()
                    tt(pa_q[:, 3, :], lre, lre, ALU.mult)
                    tt(pa_q[:, 4, :], lim, lim, ALU.mult)
                    step(v.tensor_scalar(pa_q[:, 5, :], pwr[:, BLK + 1, :], 1.0, None, ALU.subtract))
                    ttw(pa_q[:, 3, :], pa_q[:, 3, :], pa_q[:, 4, :], ALU.add)
                    tt(pa_q[:, 6, :], pa_q[:, 5, :], lre, ALU.mult)
                    tt(pa_q[:, 7, :], pwi[:, BLK + 1, :], lim, ALU.mult)
                    tt(pa_q[:, 8, :], pwi[:, BLK + 1, :], lre, ALU.mult)
                    tt(pa_q[:, 9, :], pa_q[:, 5, :], lim, ALU.mult)
                    step.wait()
                    step(v.reciprocal(pa_q[:, 4, :], pa_q[:, 3, :]))
                    ttw(pa_q[:, 6, :], pa_q[:, 6, :], pa_q[:, 7, :], ALU.add)
                    tt(pa_q[:, 8, :], pa_q[:, 8, :], pa_q[:, 9, :], ALU.subtract)
                    ttw(pa_q[:, 6, :], pa_q[:, 6, :], pa_q[:, 4, :], ALU.mult)
                    tt(pa_q[:, 8, :], pa_q[:, 8, :], pa_q[:, 4, :], ALU.mult)
                    step.wait()
                    qr = pa_q[:, 6, :].unsqueeze(2).broadcast_to([P, GP, CH])
                    qi = pa_q[:, 8, :].unsqueeze(2).broadcast_to([P, GP, CH])
                    br = pp[:, C_BRE:C_BRE + 256].rearrange("p (g c) -> p g c", c=CH)
                    bi = pp[:, C_BIM:C_BIM + 256].rearrange("p (g c) -> p g c", c=CH)
                    t0, t1 = (f(pa_th)[:, 0:256].rearrange("p (g c) -> p g c", c=CH) for f in (
                        lambda a: a[:, :, :].rearrange("p m g -> p (m g)"),
                        lambda a: pa_k[:, :, :].rearrange("p m g -> p (m g)")))
                    tt(bbr[:, :, :], qr, br, ALU.mult)
                    tt(t0, qi, bi, ALU.mult)
                    tt(bbi[:, :, :], qr, bi, ALU.mult)
                    tt(t1, qi, br, ALU.mult)
                    step.wait()
                    v.tensor_tensor(bbr[:, :, :], bbr[:, :, :], t0, ALU.subtract)
                    v.tensor_tensor(bbi[:, :, :], bbi[:, :, :], t1, ALU.add)
                    v.tensor_scalar(nci[:, :, :], pp[:, C_CIM:C_CIM + 256].rearrange("p (g c) -> p g c", c=CH),
                                    -1.0, None, ALU.mult).then_inc(prep_v, 1)

                def pooled(k):
                    src = ub[:, k, :, :]
                    for n in range(k + 1):
                        d = 1 << n
                        dst = (s0, s1)[n % 2][:, :, :]
                        if d < BLK:
                            tt(dst[:, d:BLK, :], src[:, d:BLK, :], src[:, 0:BLK - d, :], ALU.add)
                        m = min(d, BLK)
                        tt(dst[:, 0:m, 1:J + 4], src[:, 0:m, 1:J + 4], src[:, BLK - m:BLK, 0:J + 3], ALU.add)
                        step.wait()
                        src = dst
                    tt(src[:, :, 2:4], src[:, :, 2:4],
                       pp[:, C_RC + 16 * k:C_RC + 16 * k + 16].rearrange("p (t j) -> p t j", j=2), ALU.mult)
                    step.wait()
                    step(v.scalar_tensor_tensor(ub[:, k, :, 2:JP + 2], src[:, :, 2:JP + 2], 0.5 ** (k + 1),
                                                ub[:, k, :, 2:JP + 2], ALU.mult, ALU.subtract))
                    step.wait()
                    v.scalar_tensor_tensor(ub[:, k, :, JP + 4:J + 4], src[:, :, JP + 4:J + 4], 0.5 ** (k + 1),
                                           ub[:, k, :, JP + 4:J + 4], ALU.mult, ALU.subtract).then_inc(diff_made, 1)

                inverse(S_SUM1, l * NS, l * 6)
                for t in range(KD):
                    v.wait_ge(tile_done, LT + t + 1)
                    if t < KA:
                        for pt_, out, r in halves(ps[t % 2], ua[:, t, :], (rms[:, :],)):
                            ins = v.tensor_tensor(out, pt_, r, ALU.mult)
                        ins.then_inc(tile_free, 1)
                    else:
                        k = KD - 1 - t
                        if t == KA:
                            v.wait_ge(x_kept, 16 * KD * (l + 1))
                            step(v.memset(ub[:, :, :, 0:2], 0.0))
                            step(v.tensor_copy(ub[:, :, :, JP + 2:JP + 4].rearrange("p k t j -> p (k t) j"),
                                               pp[:, C_HIST:C_HIST + 64].rearrange("p (a j) -> p a j", j=2)))
                            step(v.memset(s0[:, :, 0:1], 0.0))
                            step(v.memset(s1[:, :, 0:1], 0.0))
                        for ch, (a, b) in (((0, 2), (0, 6)), ((2, 3), (6, 8))):
                            nt = (b - a) // (ch[1] - ch[0])
                            src = ps[t % 2][:, ch[0]:ch[1], 0:nt * J].rearrange("p c (t j) -> p c t j", j=J)
                            r = rms[:, a * J:b * J].rearrange("p (c t j) -> p c t j", t=nt, j=J)
                            dst = ub[:, k, a:b, :].rearrange("p (c t) j -> p c t j", t=nt)
                            for f, g in ((slice(0, JP), slice(2, JP + 2)), (slice(JP, J), slice(JP + 4, J + 4))):
                                ins = v.tensor_tensor(dst[:, :, :, g], src[:, :, :, f], r[:, :, :, f], ALU.mult)
                        ins.then_inc(tile_free, 1)
                        v.wait_ge(tile_free, LT + t + 1 + 2)
                        for n, e in ((0, JP), (1, J + 2)):
                            ins = v.tensor_copy(hist[:, k, :, n, :], ub[:, k, :, e:e + 2])
                        ins.then_inc(hist_made, 1)
                    ahead(t)
                    if t == 0:
                        prep()
                    if t >= KA:
                        pooled(KD - 1 - t)
                for i in range(KA):
                    k = KA - 1 - i
                    v.wait_ge(ybh_made, l * KA + i + 1)
                    for pt_, out, hi in halves(ps[i % 2], ybl[:, k, :], (f32(ybh[:, k, :]),)):
                        ins = v.scalar_tensor_tensor(out, pt_, lp[:, L_SCALE + k:L_SCALE + k + 1], hi,
                                                     ALU.mult, ALU.subtract)
                    ins.then_inc(tile_free, 1)

                def add_to_x(n, m, tile):
                    v.wait_ge(tile_done, LT + n + 1)
                    for pt_, xt in halves(ps[tile], x[:, m, :] if isinstance(m, int) else tile_of(x, m)):
                        ins = v.tensor_tensor(xt, pt_, xt, ALU.add)
                    ins.then_inc(tile_free, 1)

                def wob(m):
                    v.wait_ge(x_back[m], 16 * (l + 1))
                    add_to_x(T_WOB + m, m, m % 2)
                    if m % 2:
                        ahead(B_WOB + m // 2)

                def pre(q):
                    v.wait_ge(small_free, l * NS + S_DRIVE + 4 * q + 4 + 2)
                    rotate(step, v.tensor_tensor, dtmp, q, w, zh, 0, -1)

                def scan(q):
                    step.wait()
                    for g in range(4 * q, 4 * q + 4):
                        for ri in range(2):
                            v.tensor_tensor_scan(w[:, g, ri, 0:JP], rmag[:, g:g + 1].to_broadcast([P, JP]),
                                                      zh[:, g, ri, 0:JP], 0.0, ALU.mult, ALU.add)
                            ins = v.tensor_tensor_scan(w[:, g, ri, JP:J], rmag[:, g:g + 1].to_broadcast([P, JS]),
                                                      zh[:, g, ri, JP:J], dd[:, D_INIT + ri * GP + g:D_INIT + ri * GP + g + 1],
                                                       ALU.mult, ALU.add)
                    ins.then_inc(scan_v, 1)

                def post(q):
                    v.wait_ge(scan_v, l * 4 + q + 1)
                    rotate(step, v.tensor_tensor, dtmp, q, w, zh, 1, 1)
                    v.memset(quarter(zh, q, slice(None), slice(0, 1)), 0.0)
                    for ri in range(2):
                        ins = v.tensor_copy(quarter(zh, q, ri, slice(JP, JP + 1)),
                                            dd[:, D_INIT + ri * GP + 4 * q:D_INIT + ri * GP + 4 * q + 4].unsqueeze(2))
                    ins.then_inc(st_v, 1)

                wob(0)
                wob(1)
                v.wait_ge(rot_made, l + 1)
                v.wait_ge(dd_in, 16 * (l + 1))
                v.wait_ge(small_free, l * NS + S_SUM2 + 2)
                v.wait_ge(hist_out_s, 16 * (l + 1))
                wob(2)
                pre(0)
                wob(3)
                pre(1)
                wob(4)
                scan(0)
                wob(5)
                scan(1)
                wob(6)
                post(0)
                wob(7)
                post(1)
                for q in (2, 3):
                    v.wait_ge(pre_p, l * 2 + q - 1)
                    scan(q)
                for u in range(GP):
                    v.wait_ge(carry_done, l * GP + u + 1)
                    for n in range(2):
                        i = 2 * (u - u % 2 + n) + u % 2
                        ins = v.scalar_tensor_tensor(ublk[:, i, :], ublk[:, i, :], dd[:, D_D + i:D_D + i + 1],
                                                     sm[u % 2][:, n * J:(n + 1) * J], ALU.mult, ALU.add)
                    ins.then_inc(carry_free, 1)
                for q in range(KA):
                    v.wait_ge(z_made, l * KA + q + 1)
                    v.tensor_tensor(zlo[:, q, :], ya[:, q, :], f32(zhi[:, q, :]), ALU.subtract).then_inc(zlo_made, 1)
                for m in range(KA):
                    v.wait_ge(sig_made, l * KA + m + 1)
                    v.tensor_tensor(ya[:, m, :], ya[:, m, :], (tr, ts)[m % 2][:, :], ALU.mult).then_inc(tile_free, 1)
                    if m % 2:
                        ahead(B_GLU + m // 2)
                    v.wait_ge(yah_made, l * KA + m + 1)
                    v.tensor_tensor(yal[:, m, :], ya[:, m, :], f32(yah[:, m, :]), ALU.subtract).then_inc(ya_made, 1)
                for m in range(KD):
                    add_to_x(T_WOA + m, m, m % 2)
                    if m % 2:
                        ahead(B_WOA + m // 2)
                    low_h(m, l * 16 + 8 + m, lp[:, L_FFN:L_FFN + KD])

                def hidden(n, c, m, s, hi, lo):
                    v.wait_ge(tile_done, LT + T_FF + n + 1)
                    for pt_, out, r in halves(ps[s], tr[:, :], (rms[:, :],)):
                        ins = v.scalar_tensor_tensor(out, pt_, 0.0, r, ALU.max, ALU.mult)
                    ins.then_inc(tile_free, 1)
                    v.wait_ge(tile_free, LT + T_FF + n + 1 + 2)
                    v.tensor_tensor(ts[:, :], tr[:, :], tr[:, :], ALU.mult).then_inc(sq_v, 1)
                    split_lo(LB + B_FF + n + 2, s)
                    v.wait_ge(sq_v, l * 32 + 8 * c + m + 1)
                    v.wait_ge(ghi_made, l * 32 + 8 * c + m + 1)
                    v.tensor_tensor(lo, ts[:, :], f32(hi), ALU.subtract).then_inc(hid_made, 1)

                inverse(S_SUM2, l * NS, l * 6 + 3)
                for m in range(KD):
                    hidden(m, 0, m, m % 2, ghi[:, m, :], glo[:, m, :])
                with v.Fori(0, FFC - 1) as c:
                    with v.Fori(0, KD // 2) as m2:
                        for odd in range(2):
                            n = 16 * c + 8 + 2 * m2 + odd
                            add_to_x(T_FF + n, 2 * m2 + odd, odd)
                            split_lo(LB + B_FF + n + 2, odd)
                    with v.Fori(0, KD // 2) as m2:
                        for odd in range(2):
                            m = 2 * m2 + odd
                            hidden(16 * c + 16 + m, c + 1, m, odd, tile_of(ghi, m), tile_of(glo, m))
                for m in range(KD):
                    n = 16 * (FFC - 1) + 8 + m
                    add_to_x(T_FF + n, m, m % 2)
                    split_lo(LB + B_FF + n + 2, m % 2)
                    low_h(m, l * 16 + 16 + m, lp[:, L_NEXT:L_NEXT + KD])
                step.leave(LAYERS, DVE_STEPS)

            inverse(S_SUM1, LAYERS * NS, LAYERS * 6)
            v.wait_ge(x_kept, 16 * KD * (LAYERS + 1))
            for m in range(KD):
                v.scalar_tensor_tensor(x[:, m, :], x[:, m, :], lp[:, L_NEXT + m:L_NEXT + m + 1], rms[:, :],
                                       ALU.mult, ALU.mult).then_inc(y_made, 1)

        @block.gpsimd
        def _(pool):
            step = Steps(pool, pool_s)

            def add_squares(phase_no):
                for m in range(1, KD):
                    pool.wait_ge(sq_made, 8 * phase_no + m + 1)
                    if m > 1:
                        pool.wait_ge(sq_added, 7 * phase_no + m - 1)
                    pool.tensor_tensor(rms[:, :], rms[:, :], (tr, ts)[m % 2][:, :], ALU.add).then_inc(sq_added, 1)

            pool.wait_ge(zero_set, 1)
            pool.dma_start(k_dram[:, :, 0:112], zero[:, :].unsqueeze(1).broadcast_to([CH, GROUPS, 112])).then_inc(k_zero, 16)
            pool.wait_ge(k_zero, 16)
            add_squares(0)

            with pool.Fori(0, LAYERS) as l:
                step.enter(l, POOL_STEPS)

                def tt(out, a, b, op):
                    step(pool.tensor_tensor(out, a, b, op))

                def of(dram):
                    return dram[bass.ds(l, 1)].rearrange("a p n -> (a p) n")

                pool.wait_ge(tile_free, l * NT + 2)
                pool.wait_ge(h_made, l * 16 + 8)
                pool.sem_inc(pool_passed, 1)
                pool.dma_start(pp[:, :], of(prep_in)).then_inc(pp_in, 16)
                pool.dma_start(lp[:, :], of(layer_in)).then_inc(lp_in, 16)
                pool.wait_ge(sq_added, 14 * l + 7)
                pool.sem_inc(pool_passed, 1)
                pool.dma_start(wp[:, :, :].rearrange("p k d -> p (k d)"), of(w_pool)).then_inc(wp_in, 16)
                pool.wait_ge(prep_v, l * 2 + 2)
                cr = pp[:, C_CRE:C_CRE + 256].rearrange("p (g c) -> p g c", c=CH)
                ci = pp[:, C_CIM:C_CIM + 256].rearrange("p (g c) -> p g c", c=CH)
                for q in range(4):
                    def powers(a, n):
                        return (t[:, a:a + n, 4 * q:4 * q + 4].rearrange("p m g -> p g m").unsqueeze(3)
                                .broadcast_to([P, 4, n, CH]) for t in (pwr, pwi))

                    def many(a, n):
                        return a[:, 4 * q:4 * q + 4, :].unsqueeze(2).broadcast_to([P, 4, n, CH])

                    def products(n):
                        return (pt[:, i, 0:4 * n * CH].rearrange("p (g m c) -> p g m c", m=n, c=CH)
                                for i in range(2))
                    if q:
                        pool.wait_ge(small_done, l * NS + S_PREP + 4 * q - 2)
                    pr, pi = powers(0, BLK)
                    t0, t1 = products(BLK)
                    for ri, (u, w_, op) in enumerate(((bbr, bbi, ALU.subtract), (bbi, bbr, ALU.add))):
                        step.wait()
                        tt(t0, pr, many(u, BLK), ALU.mult)
                        tt(t1, pi, many(w_, BLK), ALU.mult)
                        step.wait()
                        if ri == 0:
                            tt(xq[:, ri, :, :, :], t0, t1, op)
                    pool.tensor_tensor(xq[:, ri, :, :, :], t0, t1, op).then_inc(x_quart, 1)
                    pool.wait_ge(x_quart, l * 4 + q + 1)
                    if q:
                        pool.wait_ge(small_done, l * NS + S_PREP + 4 * q)
                        pool.wait_ge(cy_out, 32 * (l * 4 + q))
                    pr, pi = powers(BLK, BLK + 1)
                    t0, t1 = products(BLK + 1)
                    for ri, (u, w_) in enumerate(((cr, ci), (nci, cr))):
                        step.wait()
                        tt(t0, pr, many(u, BLK + 1), ALU.mult)
                        tt(t1, pi, many(w_, BLK + 1), ALU.mult)
                        step.wait()
                        if ri == 0:
                            tt(yq[:, ri, :, :, :], t0, t1, ALU.subtract)
                    pool.tensor_tensor(yq[:, ri, :, :, :], t0, t1, ALU.subtract).then_inc(y_quart, 1)
                    pool.wait_ge(y_quart, l * 4 + q + 1)
                    pool.sem_inc(pool_passed, 1)
                    for ri in range(2):
                        pool.dma_start(cy_dram[:, 4 * q:4 * q + 4, ri, :],
                                       yq[:, ri, :, 1:BLK + 1, :].rearrange("p g m c -> p g (m c)")).then_inc(cy_out, 16)
                for t in range(KA):
                    pool.wait_ge(tile_free, l * NT + t + 1 + 2)
                    pool.sem_inc(pool_passed, 1)
                    pool.dma_start(ua_dram[t * P:(t + 1) * P].rearrange("a t j -> a (t j)"), ua[:, t, :]).then_inc(ua_out, 16)
                pool.wait_ge(ua_out, 64 * (l + 1))
                pool.sem_inc(pool_passed, 1)
                for tau in range(BLK):
                    pool.dma_start(ublk[CH * tau:CH * tau + CH, :, :],
                                   ua_dram[:, tau, :].rearrange("(g c) j -> c g j", c=CH)).then_inc(ublk_in, 16)
                pool.wait_ge(hist_made, l * KA + KA)
                pool.sem_inc(pool_passed, 1)
                pool.dma_start(of(pool_out), hist[:, :, :, :, :].rearrange("p k t n j -> p (k t n j)")).then_inc(hist_out_s, 16)
                pool.wait_ge(tile_done, l * NT + KD)
                pool.wait_ge(bt_out, 64 * (l + 1))
                pool.sem_inc(pool_passed, 1)
                pool.dma_start(bt[:, :, :, :], bt_dram).then_inc(bt_in, 16)
                pool.dma_start(dd[:, :], of(dstate_in)).then_inc(dd_in, 16)
                pool.wait_ge(cy_out, 128 * (l + 1))
                pool.sem_inc(pool_passed, 1)
                pool.dma_start(cy[:, :, :, :], cy_dram).then_inc(cy_in, 16)
                pool.wait_ge(k_out, 128 * (l + 1))
                pool.sem_inc(pool_passed, 1)
                for tau in range(BLK):
                    a = CH * (BLK - 1 - tau)
                    pool.dma_start(kin[CH * tau:CH * tau + CH, :, :], k_dram[:, :, a:a + P]).then_inc(kin_in, 16)
                pool.wait_ge(tile_free, l * NT + T_POOL + KA + 2)
                pool.sem_inc(pool_passed, 1)
                for m in range(KD):
                    pool.dma_start(x[:, m, :], x_hist[bass.ds(l, 1), m].rearrange("a p n -> (a p) n")).then_inc(x_back[m], 16)
                pool.wait_ge(hist_out_s, 16 * (l + 1))
                pool.sem_inc(pool_passed, 1)
                for i in range(2):
                    step(pool.tensor_copy(rot[:, i, :, 0:1], phase[:, i, :].unsqueeze(2)))
                n = 1
                while n < JP:
                    step.wait()
                    for a in range(0, GP, 8):
                        g = slice(a, a + 8)
                        t0, t1 = (ptmp[:, i, 0:8 * n].rearrange("p (g j) -> p g j", j=n) for i in range(2))
                        fr, fi = (rot[:, i, g, n - 1:n].broadcast_to([P, 8, n]) for i in range(2))
                        sr, si = (rot[:, i, g, 0:n] for i in range(2))
                        for ri, (u, w_, op) in enumerate(((sr, si, ALU.subtract), (si, sr, ALU.add))):
                            step.wait()
                            tt(t0, u, fr, ALU.mult)
                            tt(t1, w_, fi, ALU.mult)
                            step.wait()
                            if n < JP // 2 or a == 0 or ri == 0:
                                tt(rot[:, ri, g, n:2 * n], t0, t1, op)
                    n *= 2
                pool.tensor_tensor(rot[:, 1, g, JP // 2:JP], t0, t1, ALU.add).then_inc(rot_made, 1)
                pool.wait_ge(rot_made, l + 1)
                pool.wait_ge(small_free, l * NS + S_SUM2 + 2)
                for q in (2, 3):
                    rotate(step, pool.tensor_tensor, ptmp, q, w, zh, 0, -1, pre_p)
                    pool.wait_ge(pre_p, l * 2 + q - 1)
                for q in (2, 3):
                    pool.wait_ge(scan_v, l * 4 + q + 1)
                    rotate(step, pool.tensor_tensor, ptmp, q, w, zh, 1, 1)
                    pool.memset(quarter(zh, q, slice(None), slice(0, 1)), 0.0)
                    for ri in range(2):
                        ins = pool.tensor_copy(quarter(zh, q, ri, slice(JP, JP + 1)),
                                               dd[:, D_INIT + ri * GP + 4 * q:D_INIT + ri * GP + 4 * q + 4].unsqueeze(2))
                    ins.then_inc(st_p, 1)
                    pool.wait_ge(st_p, l * 2 + q - 1)
                for s, (i, j) in enumerate(((JP - 1, JP - 1), (JS - 1, J - 1))):
                    cos, sin = (rot[:, r, :, i:i + 1] for r in range(2))
                    re, im = (w[:, :, r, j:j + 1] for r in range(2))
                    t0, t1 = (ptmp[:, r, 0:GP].unsqueeze(2) for r in range(2))
                    for ri, (u, w_, op) in enumerate(((re, im, ALU.subtract), (im, re, ALU.add))):
                        if s or ri:
                            pool.wait_ge(fin_made, 4 * l + 2 * s + ri)
                        tt(t0, cos, u, ALU.mult)
                        tt(t1, sin, w_, ALU.mult)
                        step.wait()
                        pool.tensor_tensor(fin[:, s, ri, :].unsqueeze(2), t0, t1, op).then_inc(fin_made, 1)
                pool.wait_ge(fin_made, 4 * (l + 1))
                pool.sem_inc(pool_passed, 1)
                pool.dma_start(of(ssm_out), fin[:, :, :, :].rearrange("p s r g -> p (s r g)")).then_inc(fin_out, 16)
                add_squares(2 * l + 1)
                add_squares(2 * l + 2)
                step.leave(LAYERS, POOL_STEPS)


DVE_STEPS = 112
POOL_STEPS = 179


def _frames(xp, xs):
    d = xp.shape[-1]
    a = np.concatenate([xp.reshape(JP, BLK, d), xs.reshape(JS, BLK, d)], axis=0)
    return np.ascontiguousarray(a.transpose(2, 1, 0)).reshape(d // P, P, T)


def _lhs(wt, k0, n_k, m):
    return wt[k0 * P:(k0 + n_k) * P, m * P:(m + 1) * P].reshape(n_k, P, P).transpose(1, 0, 2).reshape(P, n_k * P)


def _pairs(a):
    return np.moveaxis(a.reshape(GP, 2, ST, *a.shape[2:]), 0, 2).reshape(P, GP, *a.shape[2:])


def kernel(**inputs):
    import concourse.bacc as bacc
    from concourse.bass_utils import run_bass_kernel_spmd as run

    a = {k: np.asarray(v) for k, v in inputs.items()}
    f = np.float32
    x_in = _frames(a["x_prompt"][0], a["x_sample"][0])
    blocks = []
    for l in range(LAYERS):
        w_in, w_out, w_glu = a["w_in"][l], a["w_out"][l], a["w_glu"][l]
        blocks += [_lhs(w_in, 0, KD, m) for m in (0, 1, 2, 3, 7, 6, 5, 4)]
        for wt, k0, n in ((w_out, KA, KD), (w_glu, 0, KA), (w_out, 0, KD)):
            blocks += [np.concatenate([_lhs(wt, k0, KA, m), _lhs(wt, k0, KA, m + 1)], 1) for m in range(0, n, 2)]
        for c in range(FFC):
            blocks += [_lhs(a["w_ff1"][l], 0, KD, KD * c + m) for m in range(KD)]
            blocks += [_lhs(a["w_ff2"][l], KD * c, KD, m) for m in range(KD)]
    blocks += blocks[:2]
    w_blocks = np.stack(blocks)
    w_pool = np.ascontiguousarray(a["w_pool"].transpose(0, 2, 1, 3)).reshape(LAYERS, P, KA * P)

    prep = np.zeros((LAYERS, P, NPP), f)
    ms = np.array([*range(BLK - 1, -1, -1), *range(BLK + 1)], f)
    prep[:, :, C_M:C_M + NM * GP] = np.repeat(ms, GP)
    prep[:, :, C_ID:C_ID + P] = np.eye(P, dtype=f)
    t = np.arange(2 * BLK).reshape(2, BLK).T
    for k in range(KA):
        win = 2 << k
        prep[:, :, C_RC + 16 * k:C_RC + 16 * k + 16] = (win / np.minimum(t + 1, win)).astype(f).reshape(-1)
    layer = np.zeros((LAYERS, P, NLP), f)
    dstate = np.zeros((LAYERS, P, ND), f)
    col = lambda g: g.reshape(-1, P).T
    for l in range(LAYERS):
        prep[l, :, C_LRE:C_LRE + GP] = _pairs(a["ssm_lambda_re"][l])
        prep[l, :, C_LIM:C_LIM + GP] = _pairs(a["ssm_lambda_im"][l])
        prep[l, :, C_LDT:C_LDT + GP] = _pairs(np.repeat(a["ssm_log_dt"][l][:, None], ST, 1))
        for o, name in ((C_BRE, "ssm_b_re"), (C_BIM, "ssm_b_im")):
            prep[l, :, o:o + 256] = _pairs(a[name][l]).reshape(P, 256)
        for o, name in ((C_CRE, "ssm_c_re"), (C_CIM, "ssm_c_im")):
            prep[l, :, o:o + 256] = _pairs(a[name][l].transpose(0, 2, 1)).reshape(P, 256)
        h = np.concatenate([np.zeros((1, KA * P), f), a["state_pool"][l, 0]], 0)
        prep[l, :, C_HIST:C_HIST + 64] = h.reshape(2, BLK, KA, P).transpose(3, 2, 1, 0).reshape(P, 64)
        layer[l, :, L_FFN:L_FFN + KD] = col(a["g_ffn"][l])
        layer[l, :, L_NEXT:L_NEXT + KD] = col(a["g_mix"][l + 1] if l + 1 < LAYERS else a["g_final"])
        layer[l, :, L_SCALE:L_SCALE + KA] = col(a["pool_scale"][l])
        d = a["ssm_d"][l].reshape(GROUPS, CH).T
        dstate[l, :, D_D:D_D + GROUPS] = np.tile(d, (BLK, 1))
        dstate[l, :, D_INIT:D_INIT + GP] = _pairs(a["state_ssm_re"][l, 0])
        dstate[l, :, D_INIT + GP:D_INIT + 2 * GP] = _pairs(a["state_ssm_im"][l, 0])
    gain0 = np.ascontiguousarray(col(a["g_mix"][0]))

    nc = bacc.Bacc("TRN2", target_bir_lowering=False, num_devices=1)
    arrays = {"x_t": x_in, "w_blocks": w_blocks, "w_pool_t": w_pool, "prep": prep, "gain0": gain0,
              "layer": layer, "dstate": dstate}
    args = [nc.dram_tensor(n, v.shape, F32, kind="ExternalInput").ap() for n, v in arrays.items()]
    outs = {"y_t": (KD, P, T), "pool_t": (LAYERS, P, 128), "ssm_t": (LAYERS, P, 64)}
    args += [nc.dram_tensor(n, s, F32, kind="ExternalOutput").ap() for n, s in outs.items()]
    hybrid_trunk(nc, *args)
    r = run(nc, [arrays], core_ids=[0]).results[0]

    y = r["y_t"].reshape(DM, BLK, J).transpose(2, 1, 0)
    y_prompt = np.ascontiguousarray(y[:JP]).reshape(1, SEQ, DM)
    y_sample = np.ascontiguousarray(y[JP:]).reshape(1, DSEQ, DM)
    h = r["pool_t"].reshape(LAYERS, P, KA, BLK, 2, 2).transpose(4, 0, 5, 3, 2, 1).reshape(2, LAYERS, 1, 2 * BLK, KA * P)
    h = np.ascontiguousarray(h[:, :, :, 1:])
    s = r["ssm_t"].reshape(LAYERS, 2, ST, 2, 2, GP).transpose(3, 4, 0, 5, 1, 2).reshape(2, 2, LAYERS, 1, GROUPS, ST)
    s = np.ascontiguousarray(s)
    return (y_prompt, y_sample, s[0, 0], s[0, 1], h[0], s[1, 0], s[1, 1], h[1])
```

```python
from contextlib import ExitStack

import numpy as np

import concourse.bass as bass
from concourse import mybir

F32 = mybir.dt.float32
F32R = mybir.dt.float32r
ALU = mybir.AluOpType
ACT = mybir.ActivationFunctionType

P = 128
DM = 1024
LAYERS = 2
SEQ, DSEQ = 1024, 64
BLK = 8
JP, JS = SEQ // BLK, DSEQ // BLK
J = JP + JS
T = BLK * J
KD = DM // P
KA = 4
DFF = 4 * DM
GROUPS, CH, ST = 32, 16, 64
GP = GROUPS // 2
EPS = 1e-5
CHUNKS = ((0, 3), (3, 6), (6, 8))
WIDE = 3 * J

B_WIN, B_WOB, B_GLU, B_WOA, B_FF = 0, 8, 12, 14, 18
FFC = DFF // P // KD
NB = B_FF + 2 * KD * FFC
T_WIN, T_POOL, T_WOB, T_GLU, T_WOA, T_FF = 0, 8, 12, 20, 24, 32
NT = T_FF + 2 * KD * FFC
S_SUM1, S_PREP = 0, 3
S_SUM2 = S_PREP + 32
NS = S_SUM2 + 3

NM = 17
C_LRE, C_LIM, C_LDT = 0, 16, 32
C_M = 48
C_BRE = C_M + NM * GP
C_BIM, C_CRE, C_CIM = C_BRE + 256, C_BRE + 512, C_BRE + 768
C_ID = C_BRE + 1024
C_HIST = C_ID + 128
C_RC = C_HIST + 64
NPP = C_RC + 64

L_FFN, L_NEXT, L_SCALE, NLP = 0, 8, 16, 20
D_D, D_INIT, ND = 0, 32, 64

TWO_PI = 6.283185307179586
C1 = 6.28125
C2 = 0.00193500518798828125
C3 = TWO_PI - C1 - C2
MAGIC = 12582912.0


def hybrid_trunk(nc, x_in, w_blocks, w_pool, prep_in, gain0, layer_in, dstate_in,
                 y_out, pool_out, ssm_out):
    x_hist = nc.dram_tensor("x_kept", (LAYERS + 1, KD, P, T), F32, kind="Internal").ap()
    ua_dram = nc.dram_tensor("ua_dram", (KA * P, BLK, J), F32, kind="Internal").ap()
    ya_dram = nc.dram_tensor("ya_dram", (KA * P, BLK, J), F32, kind="Internal").ap()
    cy_dram = nc.dram_tensor("cy_dram", (P, GP, 2, P), F32, kind="Internal").ap()
    k_dram = nc.dram_tensor("k_dram", (CH, GROUPS, 240), F32, kind="Internal").ap()

    with ExitStack() as ctx:
        base = ((nc.sbuf_base + 31) // 32) * 32
        words = (nc.sbuf_usable_end - base) // 4

        def at(name, offset, shape, dt=F32):
            assert offset + int(np.prod(shape[1:])) <= words, name
            return nc.alloc_sbuf_tensor_at(name, list(shape), dt, offset=base + 4 * offset)

        def sem(name):
            return ctx.enter_context(nc.semaphore(name))

        x = at("x", 0, [P, KD, T])
        ub = at("ub", 0, [P, KA, BLK, J + 4])
        s0 = at("pool_s0", 4480, [P, BLK, J + 4])
        s1 = at("pool_s1", 5600, [P, BLK, J + 4])
        xt = at("drive_products", 6720, [P, 2, 4 * J])
        wp = at("w_pool_sb", 6720 + 8 * J, [P, KA, P])
        hist = at("hist_out", 7232 + 8 * J, [P, KA, BLK, 2, 2])
        H = KD * T
        hhi = at("h_high", H, [P, KD, T], F32R)
        hlo = at("h_low", 2 * H, [P, KD, T], F32R)
        zh = at("states", H, [P, GP, 2, J])
        cy = at("carry_weights", H + 4352, [P, GP, 2, P])
        kin = at("intra_weights", H + 8448, [P, GROUPS, P])
        fin = at("final_states", H + 12544, [P, 2, 2, GP])
        rot23 = at("rotations_23", H + 13056, [P, 2, GP // 2, J])
        ptmp = at("pool_products", H + 13056 + 16 * J, [P, 2, 4 * J])
        ya = at("y_a", H + 13056, [P, KA, T])
        zhi = at("z_high", H, [P, KA, T], F32R)
        zlo = at("z_low", H + 4352, [P, KA, T], F32R)
        G = 3 * H
        ghi = at("hidden_high", G, [P, KD, T], F32R)
        glo = at("hidden_low", G + 8704, [P, KD, T], F32R)
        ua = at("u_a", G, [P, KA, T])
        w = at("drive", G, [P, GP, 2, J])
        ublk = at("u_blocks", G + 4352, [P, GROUPS, J])
        yah = at("y_a_high", G, [P, KA, T], F32R)
        yal = at("y_a_low", G + 4352, [P, KA, T], F32R)
        ybh = at("y_b_high", G + 8704, [P, KA, T], F32R)
        ybl = at("y_b_low", G + 13056, [P, KA, T], F32R)
        o = G + 8704
        pp = at("prep_in", o, [P, NPP])
        o += NPP
        pwr = at("power_re", o, [P, NM, GP])
        pwi = at("power_im", o + 272, [P, NM, GP])
        bbr = at("bbar_re", o + 544, [P, GP, CH])
        bbi = at("bbar_im", o + 800, [P, GP, CH])
        nci = at("minus_c_im", o + 1056, [P, GP, CH])
        o += 1312
        pa_mag = at("prep_mag", o, [P, NM, GP])
        pa_th = at("prep_phase", o + 272, [P, NM, GP])
        pa_k = at("prep_turns", o + 544, [P, NM, GP])
        pa_r = at("prep_reduced", o + 816, [P, NM, GP])
        pa_s = at("prep_sine", o + 1088, [P, NM, GP])
        pa_q = at("prep_small", o + 1360, [P, 12, GP])
        btst = at("bt_stage", o, [P, 4, 2, P])
        o += 1632
        xq = at("x_quarter", o, [P, 2, 4, BLK, CH])
        yq = at("y_quarter", o + 1024, [P, 2, 4, BLK + 1, CH])
        pt = at("prep_products", o + 2176, [P, 2, 576])
        kst = at("k_stage", o + 3328, [CH, 4, P])
        R = G + 2 * H
        raw = at("w_raw", R, [P, 2, 1024])
        whi = at("w_high", R + 2048, [P, 2, 1024], F32R)
        wlo = at("w_low", R + 4096, [P, 2, 1024], F32R)
        A = R + 6144
        rms = at("rms", A, [P, T])
        tr = at("work_r", A + 1088, [P, T])
        ts = at("work_s", A + 2176, [P, T])
        dtmp = at("dve_products", A, [P, 2, 4 * J])
        rot01 = at("rotations_01", A + 1088, [P, 2, GP // 2, J])
        zero = at("zeros", G + 8704 + NPP + 1312 + 1632, [CH, 112])
        S = A + 3264
        ones = at("ones", S, [P, P])
        g0 = at("gain_0", S + 128, [P, KD])
        lp = at("layer_params", S + 136, [P, NLP])
        rmag = at("decay", S + 160, [P, GP])
        phase = at("phasor", S + 176, [P, 2, GP])
        eps_col = at("epsilon", S + 208, [P, 1])
        dd = at("d_and_init", S + 216, [P, ND])

        ps = [ctx.enter_context(nc.psum_tensor(f"tile{i}", [P, 3, 512], F32)) for i in range(2)]
        sm = [ctx.enter_context(nc.psum_tensor(f"small{i}", [P, 512], F32)) for i in range(2)]

        raw_landed = [sem(f"raw_landed{i}") for i in range(2)]
        whi_made = sem("whi_made")
        wlo_made = sem("wlo_made")
        tile_done = sem("tile_done")
        tile_free = sem("tile_free")
        small_done = sem("small_done")
        small_free = sem("small_free")
        carry_done = sem("carry_done")
        carry_free = sem("carry_free")
        const_in = sem("const_in")
        x_in_s = [sem(f"x_in{i}") for i in range(KD)]
        sq_made = sem("sq_made")
        first_sq = sem("first_sq")
        sq_added = sem("sq_added")
        hhi_made = sem("hhi_made")
        h_made = sem("h_made")
        x_kept = sem("x_kept_s")
        rstd = sem("rstd")
        ones_set = sem("ones_set")
        dve = sem("dve_step")
        pool_s = sem("pool_step")
        pp_in = sem("pp_in")
        lp_in = sem("lp_in")
        prep_v = sem("prep_v")
        prep_a = sem("prep_a")
        pe_passed = sem("pe_passed")
        pool_passed = sem("pool_passed")
        x_quart = sem("x_quart")
        y_quart = sem("y_quart")
        cy_out = sem("cy_out")
        k_out = sem("k_out")
        zero_set = sem("zero_set")
        k_zero = sem("k_zero")
        ua_out = sem("ua_out")
        ublk_in = [sem(f"ublk_in{i}") for i in range(2)]
        hist_made = sem("hist_made")
        hist_out_s = sem("hist_out_s")
        diff_made = sem("diff_made")
        wp_in = sem("wp_in")
        ybh_made = sem("ybh_made")
        x_back = [sem(f"x_back{i}") for i in range(KD)]
        cy_in = sem("cy_in")
        kin_in = sem("kin_in")
        dd_in = sem("dd_in")
        rot_made = sem("rot_made")
        pre_p = sem("pre_p")
        scan_v = sem("scan_v")
        st_v = sem("st_v")
        st_p = sem("st_p")
        fin_made = sem("fin_made")
        fin_out = sem("fin_out")
        ya_out = [sem(f"ya_out{i}") for i in range(4)]
        ya_in = [sem(f"ya_in{i}") for i in range(4)]
        gelu_made = sem("gelu_made")
        z_made = sem("z_made")
        zlo_made = sem("zlo_made")
        sig_made = sem("sig_made")
        yah_made = sem("yah_made")
        ya_made = sem("ya_made")
        sq_v = sem("sq_v")
        ghi_made = sem("ghi_made")
        hid_made = sem("hid_made")
        y_made = sem("y_made")
        y_out_s = sem("y_out_s")

        def tile_of(t, m):
            return t[:, bass.ds(m, 1), :].rearrange("p a n -> p (a n)")

        def f32(ap):
            return ap.bitcast(F32)

        def halves(tile, flat, also=()):
            yield (tile[:, 0:2, 0:WIDE], flat[:, 0:2 * WIDE].rearrange("p (c n) -> p c n", c=2),
                   *(a[:, 0:2 * WIDE].rearrange("p (c n) -> p c n", c=2) for a in also))
            yield (tile[:, 2, 0:2 * J], flat[:, 2 * WIDE:T], *(a[:, 2 * WIDE:T] for a in also))

        class Steps:

            def __init__(self, eng, semaphore):
                self.eng, self.sem, self.base, self.n = eng, semaphore, 0, 0

            def __call__(self, ins):
                ins.then_inc(self.sem, 1)
                self.n += 1

            def wait(self):
                if self.n:
                    self.eng.wait_ge(self.sem, self.base + self.n)

            def enter(self, i, per_turn):
                self.saved = (self.base, self.n)
                self.base, self.n = self.base + self.n + i * per_turn, 0

            def leave(self, turns, per_turn):
                assert self.n == per_turn, (self.n, per_turn)
                self.base, self.n = self.saved[0], self.saved[1] + turns * per_turn

        def quarter(t, q, *rest):
            return t[(slice(None), slice(4 * q, 4 * q + 4), *rest)]

        def rotate(step, tensor_tensor, tmp, q, src, dst, shift, sign, told=None):
            n = J - shift
            cos, sin = (quarter((rot01, rot23)[q // 2][:, i], q % 2, slice(0, n)) for i in range(2))
            re, im = (quarter(src, q, i, slice(0, n)) for i in range(2))
            t0, t1 = (tmp[:, i, 0:4 * n].rearrange("p (g j) -> p g j", j=n) for i in range(2))
            for ri, (u, w_, op) in enumerate(((re, im, ALU.subtract if sign > 0 else ALU.add),
                                              (im, re, ALU.add if sign > 0 else ALU.subtract))):
                step.wait()
                step(tensor_tensor(t0, cos, u, ALU.mult))
                step(tensor_tensor(t1, sin, w_, ALU.mult))
                step.wait()
                ins = tensor_tensor(quarter(dst, q, ri, slice(shift, shift + n)), t0, t1, op)
                if told is not None and ri:
                    ins.then_inc(told, 1)
                else:
                    step(ins)

        def double(step, tensor_tensor, copy, tmp, rot, n, told=None):
            pairs = rot.shape[2]
            t0, t1 = (tmp[:, i, 0:pairs * n].rearrange("p (g j) -> p g j", j=n) for i in range(2))
            fr, fi = (rot[:, i, :, n - 1:n].broadcast_to([P, pairs, n]) for i in range(2))
            sr, si = (rot[:, i, :, 0:n] for i in range(2))
            for ri, (u, w_, op) in enumerate(((sr, si, ALU.subtract), (si, sr, ALU.add))):
                step.wait()
                step(tensor_tensor(t0, u, fr, ALU.mult))
                step(tensor_tensor(t1, w_, fi, ALU.mult))
                step.wait()
                step(tensor_tensor(rot[:, ri, :, n:2 * n], t0, t1, op))
            if 2 * n == JP:
                ins = copy(rot[:, :, :, JP:J], rot[:, :, :, 0:JS])
                if told is not None:
                    ins.then_inc(told, 1)
                else:
                    step(ins)

        block = ctx.enter_context(nc.Block())

        @block.sync
        def _(sp):
            sp.dma_start(g0[:, :], gain0).then_inc(const_in, 16)
            for s in range(2):
                sp.dma_start(raw[:, s, :], w_blocks[s]).then_inc(raw_landed[s], 16)
            with sp.Fori(0, LAYERS) as l:
                LT = l * NT

                def fetch(b, s):
                    sp.wait_ge(wlo_made, b - 1)
                    sp.dma_start(raw[:, s, :], w_blocks[bass.ds(b, 1)].rearrange("a p n -> (a p) n")).then_inc(raw_landed[s], 16)

                def turn(h):
                    sp.wait_ge(ua_out, 16 * (KA * l + 2 * h + 2))
                    g = GP * h
                    for tau in range(BLK):
                        sp.dma_start(ublk[CH * tau:CH * tau + CH, g:g + GP, :],
                                     ua_dram[2 * P * h:2 * P * (h + 1), tau, :].rearrange("(g c) j -> c g j", c=CH)
                                     ).then_inc(ublk_in[h], 16)

                for b in range(2, B_FF + 2):
                    fetch(l * NB + b, b % 2)
                    t = b - 4
                    if b == 6:
                        turn(0)
                    if 0 <= t < KA:
                        sp.wait_ge(tile_free, LT + t + 1 + 2)
                        sp.dma_start(ua_dram[t * P:(t + 1) * P].rearrange("a t j -> a (t j)"), ua[:, t, :]).then_inc(ua_out, 16)
                    if b == 7:
                        turn(1)
                        sp.dma_start(dd[:, :], dstate_in[bass.ds(l, 1)].rearrange("a p n -> (a p) n")).then_inc(dd_in, 16)
                    if b == B_WOB + 3:
                        sp.wait_ge(tile_done, LT + KD)
                        sp.wait_ge(cy_out, 128 * (l + 1))
                        sp.dma_start(cy[:, :, :, :], cy_dram).then_inc(cy_in, 16)
                        sp.wait_ge(k_out, 128 * (l + 1))
                        sp.wait_ge(k_zero, 16)
                        for tau in range(BLK):
                            a = CH * (BLK - 1 - tau)
                            sp.dma_start(kin[CH * tau:CH * tau + CH, :, :], k_dram[:, :, a:a + P]).then_inc(kin_in, 16)
                        sp.wait_ge(tile_free, LT + T_POOL + KA + 2)
                        for m in range(KD):
                            sp.dma_start(x[:, m, :], x_hist[bass.ds(l, 1), m].rearrange("a p n -> (a p) n")).then_inc(x_back[m], 16)
                    if b == B_GLU + 1:
                        sp.wait_ge(fin_made, 8 * (l + 1))
                        for q in range(4):
                            sp.wait_ge(ya_out[q], 16 * BLK * (l + 1))
                            sp.dma_start(ya[:, q, :], ya_dram[q * P:(q + 1) * P].rearrange("a t j -> a (t j)")).then_inc(ya_in[q], 16)
                with sp.Fori(0, (NB - B_FF) // 2) as i:
                    for s in range(2):
                        fetch(l * NB + B_FF + 2 + 2 * i + s, s)
            sp.wait_ge(raw_landed[0], 16 * (LAYERS * NB // 2 + 1))
            sp.wait_ge(raw_landed[1], 16 * (LAYERS * NB // 2 + 1))

        @block.tensor
        def _(pe):
            def product(tile, slot, half, n_k, xh, xl, ready=None, order=range(KD)):
                order = order[:n_k]
                for k in order:
                    if ready:
                        ready(k)
                    for n, (wt, xt) in enumerate(((whi, xh), (whi, xl), (wlo, xh))):
                        lhs = wt[:, slot, (half * n_k + k) * P:(half * n_k + k + 1) * P]
                        for c, (a, b) in enumerate(CHUNKS):
                            last = pe.matmul(ps[tile][:, c, 0:(b - a) * J], lhs, xt[:, k, a * J:b * J],
                                             start=(k == order[0] and n == 0), stop=(k == order[-1] and n == 2))
                last.then_inc(tile_done, 1)

            def tile_at(n):
                pe.wait_ge(tile_free, n + 1)

            def block_at(b):
                pe.wait_ge(wlo_made, b + 1)

            def small_at(n):
                pe.wait_ge(small_free, n + 1)

            def sum_part(s, c, first, phase_no):
                a, b = CHUNKS[c]
                small_at(first + s + c)
                pe.wait_ge(sq_added, 7 * phase_no + 7)
                pe.matmul(sm[(s + c) % 2][:, 0:(b - a) * J], ones[:, :], rms[:, a * J:b * J],
                          start=True, stop=True).then_inc(small_done, 1)

            pe.wait_ge(ones_set, 1)
            with pe.Fori(0, LAYERS) as l:
                LB, LT, LS = l * NB, l * NT, l * NS

                def prep(q):
                    s = S_PREP + 8 * q
                    pe.wait_ge(x_quart, l * 4 + q + 1)
                    for ri in range(2):
                        small_at(LS + s + ri)
                        for g in range(4):
                            mm = pe.transpose(sm[(s + ri) % 2][:, g * P:(g + 1) * P],
                                              xq[:, ri, g, :, :].rearrange("p t c -> p (t c)"),
                                              pp[:, C_ID:C_ID + P])
                        mm.then_inc(small_done, 1)
                    pe.wait_ge(y_quart, l * 4 + q + 1)
                    for gl in range(2):
                        small_at(LS + s + 2 + gl)
                        pe.sem_inc(pe_passed, 1)
                        rows = slice(ST * gl, ST * gl + ST)
                        for g in range(4):
                            for ri, b in enumerate((bbr, bbi)):
                                mm = pe.matmul(sm[(s + gl) % 2][0:CH, g * P:(g + 1) * P], b[rows, 4 * q + g, :],
                                               yq[rows, ri, g, 0:BLK, :].rearrange("p t c -> p (t c)"),
                                               start=(ri == 0), stop=(ri == 1))
                        mm.then_inc(small_done, 1)

                def drives(q):
                    pe.wait_ge(ublk_in[q // 2], 16 * BLK * (l + 1))
                    pe.wait_ge(small_free, LS + S_PREP + 8 * q + 2 + 2)
                    for g in range(4):
                        n = S_PREP + 8 * q + 4 + g
                        small_at(LS + n)
                        for gl in range(2):
                            for ri in range(2):
                                mm = pe.matmul(sm[n % 2][ST * gl:ST * gl + ST, ri * J:(ri + 1) * J],
                                               btst[:, g, ri, ST * gl:ST * gl + ST],
                                               ublk[:, 2 * (4 * q + g) + gl, :], start=True, stop=True)
                        mm.then_inc(small_done, 1)

                for t in range(KD):
                    tile_at(LT + t)
                    block_at(LB + t)

                    def ready(k):
                        if t == 0:
                            pe.wait_ge(h_made, l * 16 + k + 1)
                        if t == 1 and k == 1:
                            sum_part(S_SUM1, 0, LS, 2 * l)
                            sum_part(S_SUM1, 1, LS, 2 * l)
                        if t == 1 and k == 4:
                            sum_part(S_SUM1, 2, LS, 2 * l)
                    product(t % 2, t % 2, 0, KD, hhi, hlo, ready)
                    if t >= 4:
                        drives(t - 4)
                    if 3 <= t < 7:
                        prep(t - 3)
                pe.wait_ge(wp_in, 16 * (l + 1))
                for i in range(KA):
                    k = KA - 1 - i
                    tile_at(LT + T_POOL + i)
                    pe.wait_ge(diff_made, l * KA + i + 1)
                    for c, (a, b) in enumerate(CHUNKS):
                        out = ps[i % 2][:, c, 0:(b - a) * J].rearrange("p (t j) -> p t j", j=J)
                        pe.matmul(out[:, :, 0:JP], wp[:, k, :], ub[:, k, a:b, 2:2 + JP], start=True, stop=True)
                        mm = pe.matmul(out[:, :, JP:J], wp[:, k, :], ub[:, k, a:b, JP + 4:J + 4],
                                       start=True, stop=True)
                    mm.then_inc(tile_done, 1)

                def half_tile(b0, t0, n, xh, xl, ready=None, order=range(KA)):
                    if n % 2 == 0:
                        block_at(LB + b0 + n // 2)
                    tile_at(LT + t0 + n)
                    product(n % 2, n // 2 % 2, n % 2, KA, xh, xl, ready, order)

                def wob(n):
                    half_tile(B_WOB, T_WOB, n, ybh, ybl, None if n else
                              lambda k: pe.wait_ge(tile_free, LT + T_POOL + KA - k + 2), range(KA - 1, -1, -1))

                def carry(q):
                    if q == 0:
                        pe.wait_ge(small_free, LS + S_SUM2 + 2)
                        pe.wait_ge(kin_in, 16 * BLK * (l + 1))
                        pe.wait_ge(cy_in, 16 * (l + 1))
                    sem_, n = {0: (st_p, 1), 1: (st_v, 1), 2: (st_v, 2), 3: (st_p, 2)}[q]
                    pe.wait_ge(sem_, l * 2 + n)
                    for u in range(4 * q, 4 * q + 4):
                        if u >= 2:
                            pe.wait_ge(carry_free, l * GP + u - 1)
                        gl = u % 2
                        rows = slice(ST * gl, ST * gl + ST)
                        for i in range(2):
                            g = u - gl + i
                            out = sm[gl][:, i * J:(i + 1) * J]
                            pe.matmul(out, kin[:, 2 * g + gl, :], ublk[:, 2 * g + gl, :], start=True, stop=False)
                            pe.matmul(out, cy[rows, g, 0, :], zh[rows, g, 0, :], start=False, stop=False)
                            mm = pe.matmul(out, cy[rows, g, 1, :], zh[rows, g, 1, :], start=False, stop=True)
                        mm.then_inc(carry_done, 1)

                for n in range(5):
                    wob(n)
                carry(0)
                carry(1)
                wob(5)
                carry(2)
                carry(3)
                wob(6)
                wob(7)
                for n in range(KA):
                    half_tile(B_GLU, T_GLU, n, zhi, zlo, None if n else lambda k: pe.wait_ge(zlo_made, l * KA + k + 1))
                for n in range(KD):
                    half_tile(B_WOA, T_WOA, n, yah, yal, None if n else lambda k: pe.wait_ge(ya_made, l * KA + k + 1))

                def ff_tile(slot, n, xh, xl, ready=None):
                    tile_at(LT + T_FF + n)
                    block_at(LB + B_FF + n)
                    product(slot, slot, 0, KD, xh, xl, ready)

                def ff2(c, m, odd):
                    ff_tile(odd, 16 * c + 8 + m, ghi, glo,
                            None if odd else lambda k: pe.wait_ge(hid_made, l * 32 + 8 * c + k + 1))

                pe.wait_ge(carry_free, l * GP + GP)
                for m in range(KD):
                    def ready(k):
                        if m == 0:
                            pe.wait_ge(h_made, l * 16 + 8 + k + 1)
                        if m == 1 and k == 2:
                            sum_part(S_SUM2, 2, LS, 2 * l + 1)
                    ff_tile(m % 2, m, hhi, hlo, ready)
                    if m == 0:
                        sum_part(S_SUM2, 0, LS, 2 * l + 1)
                        sum_part(S_SUM2, 1, LS, 2 * l + 1)
                with pe.Fori(0, FFC - 1) as c:
                    with pe.Fori(0, KD // 2) as m2:
                        for odd in range(2):
                            ff2(c, 2 * m2 + odd, odd)
                    with pe.Fori(0, KD // 2) as m2:
                        for odd in range(2):
                            ff_tile(odd, 16 * c + 16 + 2 * m2 + odd, hhi, hlo)
                for m in range(KD):
                    ff2(FFC - 1, m, m % 2)
            for c in range(3):
                sum_part(S_SUM1, c, LAYERS * NS, 2 * LAYERS)

        @block.scalar
        def _(act):
            act.sem_inc(small_free, 2)

            def split_hi(b, s):
                act.wait_ge(raw_landed[s], 16 * (b + 1))
                act.activation(whi[:, s, :], raw[:, s, :], ACT.Copy).then_inc(whi_made, 1)

            def finish(m, phase_no, gain, keep):
                if m > 2:
                    act.wait_ge(sq_added, 7 * phase_no + m - 2)
                dst = (tr, ts)[m % 2] if m else rms
                act.activation(dst[:, :], x[:, m, :], ACT.Square).then_inc(sq_made, 1)
                act.activation(hhi[:, m, :], x[:, m, :], ACT.Copy, scale=gain[:, m:m + 1]).then_inc(hhi_made, 1)
                if keep is not None:
                    act.dma_start(keep, x[:, m, :]).then_inc(x_kept, 16)

            def roots(s, first):
                for c, (a, b) in enumerate(CHUNKS):
                    act.wait_ge(small_done, first + s + c + 1)
                    act.activation(rms[:, a * J:b * J], sm[(s + c) % 2][:, 0:(b - a) * J], ACT.Sqrt,
                                   scale=1.0 / DM, bias=eps_col[:, :]).then_inc(small_free, 1)

            for m in range(KD):
                act.dma_start(x[:, m, :], x_in[m]).then_inc(x_in_s[m], 16)
            split_hi(0, 0)
            act.wait_ge(const_in, 16)
            for m in range(KD):
                act.wait_ge(x_in_s[m], 16)
                if m % 2 == 0:
                    if m > 2:
                        act.wait_ge(sq_added, m - 2)
                    act.activation((tr if m else rms)[:, :], x[:, m, :], ACT.Square).then_inc(sq_made, 1)
                act.activation(hhi[:, m, :], x[:, m, :], ACT.Copy, scale=g0[:, m:m + 1]).then_inc(hhi_made, 1)
                act.dma_start(x_hist[0, m], x[:, m, :]).then_inc(x_kept, 16)
            split_hi(0, 1)
            act.wait_ge(ones_set, 1)

            with act.Fori(0, LAYERS) as l:
                LB, LT, LS = l * NB, l * NT, l * NS

                def ahead(b, t):
                    act.wait_ge(tile_done, LT + t + 1)
                    split_hi(l * (NB // 2) + b // 2 + 1, b % 2)

                def prep(q):
                    s = S_PREP + 8 * q
                    for ri in range(2):
                        act.wait_ge(small_done, LS + s + ri + 1)
                        act.activation(btst[:, :, ri, :], sm[(s + ri) % 2][:, :].rearrange("p (g n) -> p g n", n=P),
                                       ACT.Copy).then_inc(small_free, 1)
                    for hb in range(2):
                        act.wait_ge(small_done, LS + s + 2 + hb + 1)
                        if q or hb:
                            act.wait_ge(k_out, 16 * (l * 8 + 2 * q + hb))
                        act.activation(kst[:, :, :], sm[(s + hb) % 2][0:CH, :].rearrange("p (g n) -> p g n", n=P),
                                       ACT.Copy).then_inc(small_free, 1)
                        act.wait_ge(small_free, LS + s + 2 + hb + 1 + 2)
                        act.dma_start(k_dram[:, 8 * q + hb:8 * q + 8:2, 112:240], kst[:, :, :]).then_inc(k_out, 16)

                def drives(q):
                    act.wait_ge(ua_out, 16 * KA * (l + 1))
                    for g in range(4 * q, 4 * q + 4):
                        n = S_PREP + 4 * q + 4 + g
                        act.wait_ge(small_done, LS + n + 1)
                        act.activation(w[:, g, :, :], sm[n % 2][:, 0:2 * J].rearrange("p (r j) -> p r j", j=J),
                                       ACT.Copy).then_inc(small_free, 1)

                def carry_weights(q):
                    act.wait_ge(y_quart, l * 4 + q + 1)
                    for ri in range(2):
                        act.dma_start(cy_dram[:, 4 * q:4 * q + 4, ri, :],
                                      yq[:, ri, :, 1:BLK + 1, :].rearrange("p g m c -> p g (m c)")).then_inc(cy_out, 16)

                roots(S_SUM1, LS)
                ahead(0, 0)
                act.wait_ge(pp_in, 16 * (l + 1))
                act.activation(pa_q[:, 0, :], pp[:, C_LDT:C_LDT + GP], ACT.Exp).then_inc(prep_a, 1)
                act.wait_ge(prep_v, l * 2 + 1)
                act.activation(pa_mag[:, :, :], pa_mag[:, :, :], ACT.Exp).then_inc(prep_a, 1)
                act.activation(pa_s[:, :, :], pa_r[:, :, :], ACT.Sin).then_inc(prep_a, 1)
                act.activation(pa_k[:, :, :], pa_r[:, :, :], ACT.Sin, scale=0.5).then_inc(prep_a, 1)
                for t in range(1, KD):
                    ahead(t, t)
                    if t >= 4:
                        drives(t - 4)
                    if 3 <= t < 7:
                        prep(t - 3)
                        carry_weights(t - 3)
                act.wait_ge(hist_made, l * KA + KA)
                act.dma_start(pool_out[bass.ds(l, 1)].rearrange("a p n -> (a p) n"),
                              hist[:, :, :, :, :].rearrange("p k t n j -> p (k t n j)")).then_inc(hist_out_s, 16)
                act.wait_ge(k_out, 128 * (l + 1))
                act.wait_ge(cy_out, 128 * (l + 1))
                act.wait_ge(lp_in, 16 * (l + 1))
                for i in range(KA):
                    k = KA - 1 - i
                    act.wait_ge(tile_done, LT + T_POOL + i + 1)
                    if i == 2:
                        act.wait_ge(diff_made, l * KA + KA)
                    for pt_, out in halves(ps[i % 2], ybh[:, k, :]):
                        ins = act.activation(out, pt_, ACT.Copy, scale=lp[:, L_SCALE + k:L_SCALE + k + 1])
                    ins.then_inc(ybh_made, 1)
                ahead(B_WOB, T_WOB + 1)
                ahead(B_WOB + 1, T_WOB + 3)

                def store(q):
                    act.wait_ge(carry_free, l * GP + 4 * q + 4)
                    for tau in range(BLK):
                        act.dma_start(ya_dram[q * P:(q + 1) * P, tau, :].rearrange("(g c) j -> c g j", c=CH),
                                      ublk[CH * tau:CH * tau + CH, 8 * q:8 * q + 8, :]).then_inc(ya_out[q], 16)

                store(0)
                store(1)
                ahead(B_WOB + 2, T_WOB + 5)
                store(2)
                store(3)
                for q in range(4):
                    act.wait_ge(ya_in[q], 16 * (l + 1))
                    act.activation(ya[:, q, :], ya[:, q, :], ACT.Gelu_apprx_tanh).then_inc(gelu_made, 1)
                    act.wait_ge(gelu_made, l * KA + q + 1)
                    act.activation(zhi[:, q, :], ya[:, q, :], ACT.Copy).then_inc(z_made, 1)
                ahead(B_WOB + 3, T_WOB + 7)
                act.wait_ge(fin_out, 16 * (l + 1))
                for m in range(KA):
                    act.wait_ge(tile_done, LT + T_GLU + m + 1)
                    for pt_, out in halves(ps[m % 2], (tr, ts)[m % 2][:, :]):
                        ins = act.activation(out, pt_, ACT.Sigmoid)
                    ins.then_inc(sig_made, 1)
                    if m % 2:
                        ahead(B_GLU + m // 2, T_GLU + m)
                    act.wait_ge(tile_free, LT + T_GLU + m + 1 + 2)
                    act.activation(yah[:, m, :], ya[:, m, :], ACT.Copy).then_inc(yah_made, 1)
                for m in range(KD):
                    act.wait_ge(tile_free, LT + T_WOA + m + 1 + 2)
                    finish(m, 2 * l + 1, lp[:, L_FFN:L_FFN + KD], None)
                    if m % 2:
                        ahead(B_WOA + m // 2, T_WOA + m)

                def hidden(n, c, out):
                    act.wait_ge(tile_free, LT + T_FF + 16 * c + n + 1 + 2)
                    act.activation(out, tr[:, :], ACT.Square).then_inc(ghi_made, 1)

                def ahead_ff(c, n, m2, odd):
                    act.wait_ge(tile_done, LT + T_FF + 16 * c + n + 2 * m2 + odd + 1)
                    split_hi(l * (NB // 2) + (B_FF + n) // 2 + 8 * c + m2 + 1, odd)

                roots(S_SUM2, LS)
                for m in range(KD):
                    hidden(m, 0, ghi[:, m, :])
                    ahead_ff(0, 0, m // 2, m % 2)
                with act.Fori(0, FFC - 1) as c:
                    with act.Fori(0, KD // 2) as m2:
                        for odd in range(2):
                            ahead_ff(c, 8, m2, odd)
                    with act.Fori(0, KD // 2) as m2:
                        for odd in range(2):
                            m = 2 * m2 + odd
                            hidden(m, c + 1, tile_of(ghi, m))
                            ahead_ff(c, 16, m2, odd)
                for m in range(KD):
                    act.wait_ge(tile_free, LT + T_FF + 16 * (FFC - 1) + 8 + m + 1 + 2)
                    finish(m, 2 * l + 2, lp[:, L_NEXT:L_NEXT + KD], x_hist[bass.ds(l + 1, 1), m].rearrange("a p n -> (a p) n"))
                    ahead_ff(FFC - 1, 8, m // 2, m % 2)

            roots(S_SUM1, LAYERS * NS)
            for m in range(KD):
                act.wait_ge(y_made, m + 1)
                act.dma_start(y_out[m], x[:, m, :]).then_inc(y_out_s, 16)
            act.wait_ge(y_out_s, 16 * KD)
            act.wait_ge(x_kept, 16 * KD * (LAYERS + 1))
            act.wait_ge(hist_out_s, 16 * LAYERS)
            act.wait_ge(fin_out, 16 * LAYERS)

        @block.vector
        def _(v):
            step = Steps(v, dve)
            v.sem_inc(tile_free, 2)

            def split_lo(b, s):
                v.wait_ge(whi_made, b + 1)
                v.tensor_tensor(wlo[:, s, :], raw[:, s, :], f32(whi[:, s, :]), ALU.subtract).then_inc(wlo_made, 1)

            def low_h(m, n, gain):
                v.wait_ge(hhi_made, n + 1)
                v.scalar_tensor_tensor(hlo[:, m, :], x[:, m, :], gain[:, m:m + 1], f32(hhi[:, m, :]),
                                       ALU.mult, ALU.subtract).then_inc(h_made, 1)

            def inverse(s, first, n):
                for c, (a, b) in enumerate(CHUNKS):
                    v.wait_ge(small_free, first + s + c + 1 + 2)
                    v.reciprocal(rms[:, a * J:b * J], rms[:, a * J:b * J]).then_inc(rstd, 1)
                v.wait_ge(rstd, n + 3)

            v.memset(eps_col[:, :], EPS)
            v.memset(ones[:, :], 1.0).then_inc(ones_set, 1)
            v.memset(zero[:, :], 0.0).then_inc(zero_set, 1)
            split_lo(0, 0)
            v.wait_ge(const_in, 16)
            for m in range(KD):
                v.wait_ge(x_in_s[m], 16)
                if m % 2:
                    if m > 2:
                        v.wait_ge(sq_added, m - 2)
                    v.tensor_tensor(ts[:, :], x[:, m, :], x[:, m, :], ALU.mult).then_inc(first_sq, 1)
                low_h(m, m, g0)
            split_lo(1, 1)

            with v.Fori(0, LAYERS) as l:
                LB, LT = l * NB, l * NT
                step.enter(l, DVE_STEPS)

                def ahead(b):
                    split_lo(LB + b + 2, b % 2)

                def tt(out, a, b, op):
                    step(v.tensor_tensor(out, a, b, op))

                def ttw(out, a, b, op):
                    step.wait()
                    tt(out, a, b, op)

                def over(ap, n):
                    return ap.unsqueeze(1).broadcast_to([P, n, GP])

                def angles():
                    lre, lim = pp[:, C_LRE:C_LRE + GP], pp[:, C_LIM:C_LIM + GP]
                    ms = pp[:, C_M:C_M + NM * GP].rearrange("p (m g) -> p m g", g=GP)
                    v.wait_ge(prep_a, l * 4 + 1)
                    tt(pa_q[:, 1, :], lre, pa_q[:, 0, :], ALU.mult)
                    tt(pa_q[:, 2, :], lim, pa_q[:, 0, :], ALU.mult)
                    step.wait()
                    tt(pa_mag[:, :, :], ms, over(pa_q[:, 1, :], NM), ALU.mult)
                    tt(pa_th[:, :, :], ms, over(pa_q[:, 2, :], NM), ALU.mult)
                    step.wait()
                    step(v.tensor_scalar(pa_k[:, :, :], pa_th[:, :, :], 1.0 / TWO_PI, MAGIC, ALU.mult, ALU.add))
                    step.wait()
                    step(v.tensor_scalar(pa_k[:, :, :], pa_k[:, :, :], MAGIC, None, ALU.subtract))
                    step.wait()
                    step(v.scalar_tensor_tensor(pa_r[:, :, :], pa_k[:, :, :], -C1, pa_th[:, :, :], ALU.mult, ALU.add))
                    step.wait()
                    step(v.scalar_tensor_tensor(pa_r[:, :, :], pa_k[:, :, :], -C2, pa_r[:, :, :], ALU.mult, ALU.add))
                    step.wait()
                    step(v.scalar_tensor_tensor(pa_r[:, :, :], pa_k[:, :, :], -C3, pa_r[:, :, :], ALU.mult, ALU.add))
                    step.wait()
                    v.tensor_scalar(pa_r[:, :, :], pa_r[:, :, :], 3.1415925, -3.1415925, ALU.min,
                                    ALU.max).then_inc(prep_v, 1)

                def discretised():
                    lre, lim = pp[:, C_LRE:C_LRE + GP], pp[:, C_LIM:C_LIM + GP]
                    v.wait_ge(prep_a, l * 4 + 4)
                    tt(pa_th[:, :, :], pa_k[:, :, :], pa_k[:, :, :], ALU.mult)
                    step.wait()
                    step(v.tensor_scalar(pa_th[:, :, :], pa_th[:, :, :], -2.0, 1.0, ALU.mult, ALU.add))
                    step.wait()
                    tt(pwr[:, :, :], pa_mag[:, :, :], pa_th[:, :, :], ALU.mult)
                    tt(pwi[:, :, :], pa_mag[:, :, :], pa_s[:, :, :], ALU.mult)
                    step(v.tensor_copy(rmag[:, :], pa_mag[:, NM - 1, :]))
                    step(v.tensor_copy(phase[:, 0, :], pa_th[:, NM - 1, :]))
                    step(v.tensor_copy(phase[:, 1, :], pa_s[:, NM - 1, :]))
                    step.wait()
                    tt(pa_q[:, 3, :], lre, lre, ALU.mult)
                    tt(pa_q[:, 4, :], lim, lim, ALU.mult)
                    step(v.tensor_scalar(pa_q[:, 5, :], pwr[:, BLK + 1, :], 1.0, None, ALU.subtract))
                    ttw(pa_q[:, 3, :], pa_q[:, 3, :], pa_q[:, 4, :], ALU.add)
                    tt(pa_q[:, 6, :], pa_q[:, 5, :], lre, ALU.mult)
                    tt(pa_q[:, 7, :], pwi[:, BLK + 1, :], lim, ALU.mult)
                    tt(pa_q[:, 8, :], pwi[:, BLK + 1, :], lre, ALU.mult)
                    tt(pa_q[:, 9, :], pa_q[:, 5, :], lim, ALU.mult)
                    step.wait()
                    step(v.reciprocal(pa_q[:, 4, :], pa_q[:, 3, :]))
                    ttw(pa_q[:, 6, :], pa_q[:, 6, :], pa_q[:, 7, :], ALU.add)
                    tt(pa_q[:, 8, :], pa_q[:, 8, :], pa_q[:, 9, :], ALU.subtract)
                    ttw(pa_q[:, 6, :], pa_q[:, 6, :], pa_q[:, 4, :], ALU.mult)
                    tt(pa_q[:, 8, :], pa_q[:, 8, :], pa_q[:, 4, :], ALU.mult)
                    step.wait()
                    qr = pa_q[:, 6, :].unsqueeze(2).broadcast_to([P, GP, CH])
                    qi = pa_q[:, 8, :].unsqueeze(2).broadcast_to([P, GP, CH])
                    br = pp[:, C_BRE:C_BRE + 256].rearrange("p (g c) -> p g c", c=CH)
                    bi = pp[:, C_BIM:C_BIM + 256].rearrange("p (g c) -> p g c", c=CH)
                    t0, t1 = (f(pa_th)[:, 0:256].rearrange("p (g c) -> p g c", c=CH) for f in (
                        lambda a: a[:, :, :].rearrange("p m g -> p (m g)"),
                        lambda a: pa_k[:, :, :].rearrange("p m g -> p (m g)")))
                    tt(bbr[:, :, :], qr, br, ALU.mult)
                    tt(t0, qi, bi, ALU.mult)
                    tt(bbi[:, :, :], qr, bi, ALU.mult)
                    tt(t1, qi, br, ALU.mult)
                    step.wait()
                    v.tensor_tensor(bbr[:, :, :], bbr[:, :, :], t0, ALU.subtract)
                    v.tensor_tensor(bbi[:, :, :], bbi[:, :, :], t1, ALU.add)
                    v.tensor_scalar(nci[:, :, :], pp[:, C_CIM:C_CIM + 256].rearrange("p (g c) -> p g c", c=CH),
                                    -1.0, None, ALU.mult).then_inc(prep_v, 1)

                def drive_weights(q):
                    v.wait_ge(prep_v, l * 2 + 2)
                    if q:
                        v.wait_ge(small_done, l * NS + S_PREP + 8 * q - 6)
                    pr, pi = (t[:, 0:BLK, 4 * q:4 * q + 4].rearrange("p m g -> p g m").unsqueeze(3)
                              .broadcast_to([P, 4, BLK, CH]) for t in (pwr, pwi))
                    br, bi = (t[:, 4 * q:4 * q + 4, :].unsqueeze(2).broadcast_to([P, 4, BLK, CH]) for t in (bbr, bbi))
                    t0, t1 = (xt[:, i, 0:4 * BLK * CH].rearrange("p (g m c) -> p g m c", m=BLK, c=CH) for i in range(2))
                    for ri, (a, b, op) in enumerate(((br, bi, ALU.subtract), (bi, br, ALU.add))):
                        step.wait()
                        tt(t0, pr, a, ALU.mult)
                        tt(t1, pi, b, ALU.mult)
                        step.wait()
                        if ri == 0:
                            tt(xq[:, ri, :, :, :], t0, t1, op)
                    v.tensor_tensor(xq[:, 1, :, :, :], t0, t1, ALU.add).then_inc(x_quart, 1)
                    v.wait_ge(x_quart, l * 4 + q + 1)

                def pooled(k):
                    src = ub[:, k, :, :]
                    for n in range(k + 1):
                        d = 1 << n
                        dst = (s0, s1)[n % 2][:, :, :]
                        if d < BLK:
                            tt(dst[:, d:BLK, :], src[:, d:BLK, :], src[:, 0:BLK - d, :], ALU.add)
                        m = min(d, BLK)
                        tt(dst[:, 0:m, 1:J + 4], src[:, 0:m, 1:J + 4], src[:, BLK - m:BLK, 0:J + 3], ALU.add)
                        step.wait()
                        src = dst
                    tt(src[:, :, 2:4], src[:, :, 2:4],
                       pp[:, C_RC + 16 * k:C_RC + 16 * k + 16].rearrange("p (t j) -> p t j", j=2), ALU.mult)
                    step.wait()
                    step(v.scalar_tensor_tensor(ub[:, k, :, 2:JP + 2], src[:, :, 2:JP + 2], 0.5 ** (k + 1),
                                                ub[:, k, :, 2:JP + 2], ALU.mult, ALU.subtract))
                    step.wait()
                    v.scalar_tensor_tensor(ub[:, k, :, JP + 4:J + 4], src[:, :, JP + 4:J + 4], 0.5 ** (k + 1),
                                           ub[:, k, :, JP + 4:J + 4], ALU.mult, ALU.subtract).then_inc(diff_made, 1)

                def pre(q):
                    v.wait_ge(small_free, l * NS + S_PREP + 8 * q + 8 + 2)
                    rotate(step, v.tensor_tensor, dtmp, q, w, zh, 0, -1)

                def early_pre(q):
                    v.wait_ge(small_free, l * NS + S_PREP + 8 * q + 8 + 2)
                    if q:
                        v.wait_ge(rot_made, l * 2 + 1)
                    for g in range(4 * q, 4 * q + 4, 2):
                        cos, sin = (rot01[:, i, g:g + 2, :] for i in range(2))
                        re, im = (w[:, g:g + 2, i, :] for i in range(2))
                        t = [xt[:, i // 2, 2 * J * (i % 2):2 * J * (i % 2 + 1)].rearrange("p (g j) -> p g j", j=J)
                             for i in range(4)]
                        step.wait()
                        tt(t[0], cos, re, ALU.mult)
                        tt(t[1], sin, im, ALU.mult)
                        tt(t[2], cos, im, ALU.mult)
                        tt(t[3], sin, re, ALU.mult)
                        step.wait()
                        tt(re, t[0], t[1], ALU.add)
                        tt(im, t[2], t[3], ALU.subtract)

                def scan(q, src):
                    step.wait()
                    for g in range(4 * q, 4 * q + 4):
                        for ri in range(2):
                            v.tensor_tensor_scan(w[:, g, ri, 0:JP], rmag[:, g:g + 1].to_broadcast([P, JP]),
                                                 src[:, g, ri, 0:JP], 0.0, ALU.mult, ALU.add)
                            ins = v.tensor_tensor_scan(w[:, g, ri, JP:J], rmag[:, g:g + 1].to_broadcast([P, JS]),
                                                       src[:, g, ri, JP:J], dd[:, D_INIT + ri * GP + g:D_INIT + ri * GP + g + 1],
                                                       ALU.mult, ALU.add)
                    ins.then_inc(scan_v, 1)

                def post(q):
                    v.wait_ge(scan_v, l * 4 + (1, 2, 4)[q])
                    rotate(step, v.tensor_tensor, dtmp, q, w, zh, 1, 1)
                    step.wait()
                    v.memset(quarter(zh, q, slice(None), slice(0, 1)), 0.0)
                    for ri in range(2):
                        ins = v.tensor_copy(quarter(zh, q, ri, slice(JP, JP + 1)),
                                            dd[:, D_INIT + ri * GP + 4 * q:D_INIT + ri * GP + 4 * q + 4].unsqueeze(2))
                    ins.then_inc(st_v, 1)

                inverse(S_SUM1, l * NS, l * 6)
                for t in range(KD):
                    v.wait_ge(tile_done, LT + t + 1)
                    if t < KA:
                        for pt_, out, r in halves(ps[t % 2], ua[:, t, :], (rms[:, :],)):
                            ins = v.tensor_tensor(out, pt_, r, ALU.mult)
                        ins.then_inc(tile_free, 1)
                    else:
                        k = KD - 1 - t
                        if t == KA:
                            step(v.memset(ub[:, :, :, 0:2], 0.0))
                            step(v.tensor_copy(ub[:, :, :, JP + 2:JP + 4].rearrange("p k t j -> p (k t) j"),
                                               pp[:, C_HIST:C_HIST + 64].rearrange("p (a j) -> p a j", j=2)))
                            step(v.memset(s0[:, :, 0:1], 0.0))
                            step(v.memset(s1[:, :, 0:1], 0.0))
                        for ch, (a, b) in (((0, 2), (0, 6)), ((2, 3), (6, 8))):
                            nt = (b - a) // (ch[1] - ch[0])
                            src = ps[t % 2][:, ch[0]:ch[1], 0:nt * J].rearrange("p c (t j) -> p c t j", j=J)
                            r = rms[:, a * J:b * J].rearrange("p (c t j) -> p c t j", t=nt, j=J)
                            dst = ub[:, k, a:b, :].rearrange("p (c t) j -> p c t j", t=nt)
                            for f, g in ((slice(0, JP), slice(2, JP + 2)), (slice(JP, J), slice(JP + 4, J + 4))):
                                ins = v.tensor_tensor(dst[:, :, :, g], src[:, :, :, f], r[:, :, :, f], ALU.mult)
                        ins.then_inc(tile_free, 1)
                        v.wait_ge(tile_free, LT + t + 1 + 2)
                        for n, e in ((0, JP), (1, J + 2)):
                            ins = v.tensor_copy(hist[:, k, :, n, :], ub[:, k, :, e:e + 2])
                        ins.then_inc(hist_made, 1)
                    ahead(t)
                    if t == 0:
                        angles()
                    if t == 1:
                        discretised()
                        v.wait_ge(x_kept, 16 * KD * (l + 1))
                        drive_weights(0)
                    if 3 <= t < 6:
                        drive_weights(t - 2)
                    if t == 3:
                        rot0 = rot01[:, :, 0:4, :]
                        for i in range(2):
                            step(v.tensor_copy(rot0[:, i, :, 0:1], phase[:, i, 0:4].unsqueeze(2)))
                        for n in (1, 2, 4, 8, 16, 32, 64):
                            double(step, v.tensor_tensor, v.tensor_copy, xt, rot0, n)
                    if t >= KA:
                        pooled(KD - 1 - t)
                    if t == 4:
                        early_pre(0)
                    if t == 5:
                        v.wait_ge(dd_in, 16 * (l + 1))
                        scan(0, w)
                        early_pre(1)
                    if t == 6:
                        scan(1, w)
                v.wait_ge(rot_made, l * 2 + 1)
                rot2 = rot23[:, :, 0:4, :]
                for i in range(2):
                    step(v.tensor_copy(rot2[:, i, :, 0:1], phase[:, i, 8:12].unsqueeze(2)))
                for i in range(KA):
                    k = KA - 1 - i
                    v.wait_ge(ybh_made, l * KA + i + 1)
                    if i == KA - 1:
                        v.wait_ge(hist_out_s, 16 * (l + 1))
                    for pt_, out, hi in halves(ps[i % 2], ybl[:, k, :], (f32(ybh[:, k, :]),)):
                        ins = v.scalar_tensor_tensor(out, pt_, lp[:, L_SCALE + k:L_SCALE + k + 1], hi,
                                                     ALU.mult, ALU.subtract)
                    ins.then_inc(tile_free, 1)
                    for n in ((1, 2, 4), (8,), (16,), (32, 64))[i]:
                        double(step, v.tensor_tensor, v.tensor_copy, dtmp, rot2, n)

                def add_to_x(n, m, tile):
                    v.wait_ge(tile_done, LT + n + 1)
                    for pt_, xt in halves(ps[tile], x[:, m, :] if isinstance(m, int) else tile_of(x, m)):
                        ins = v.tensor_tensor(xt, pt_, xt, ALU.add)
                    ins.then_inc(tile_free, 1)

                def wob(m):
                    v.wait_ge(x_back[m], 16 * (l + 1))
                    add_to_x(T_WOB + m, m, m % 2)
                    if m % 2 and m < 7:
                        ahead(B_WOB + m // 2)

                def output(q):
                    for u in range(4 * q, 4 * q + 4):
                        v.wait_ge(carry_done, l * GP + u + 1)
                        for n in range(2):
                            i = 2 * (u - u % 2 + n) + u % 2
                            ins = v.scalar_tensor_tensor(ublk[:, i, :], ublk[:, i, :], dd[:, D_D + i:D_D + i + 1],
                                                         sm[u % 2][:, n * J:(n + 1) * J], ALU.mult, ALU.add)
                        ins.then_inc(carry_free, 1)

                wob(0)
                pre(2)
                wob(1)
                v.wait_ge(pre_p, l + 1)
                scan(3, zh)
                scan(2, zh)
                wob(2)
                post(1)
                wob(3)
                post(2)
                wob(4)
                output(0)
                output(1)
                wob(5)
                output(2)
                output(3)
                wob(6)
                wob(7)
                for q in range(KA):
                    v.wait_ge(z_made, l * KA + q + 1)
                    v.tensor_tensor(zlo[:, q, :], ya[:, q, :], f32(zhi[:, q, :]), ALU.subtract).then_inc(zlo_made, 1)
                ahead(B_WOB + 3)
                for m in range(KA):
                    v.wait_ge(sig_made, l * KA + m + 1)
                    v.tensor_tensor(ya[:, m, :], ya[:, m, :], (tr, ts)[m % 2][:, :], ALU.mult).then_inc(tile_free, 1)
                    if m % 2:
                        ahead(B_GLU + m // 2)
                    v.wait_ge(yah_made, l * KA + m + 1)
                    v.tensor_tensor(yal[:, m, :], ya[:, m, :], f32(yah[:, m, :]), ALU.subtract).then_inc(ya_made, 1)
                for m in range(KD):
                    add_to_x(T_WOA + m, m, m % 2)
                    if m % 2:
                        ahead(B_WOA + m // 2)
                    low_h(m, l * 16 + 8 + m, lp[:, L_FFN:L_FFN + KD])

                def hidden(n, c, m, s, hi, lo):
                    v.wait_ge(tile_done, LT + T_FF + n + 1)
                    for pt_, out, r in halves(ps[s], tr[:, :], (rms[:, :],)):
                        ins = v.scalar_tensor_tensor(out, pt_, 0.0, r, ALU.max, ALU.mult)
                    ins.then_inc(tile_free, 1)
                    v.wait_ge(tile_free, LT + T_FF + n + 1 + 2)
                    v.tensor_tensor(ts[:, :], tr[:, :], tr[:, :], ALU.mult).then_inc(sq_v, 1)
                    split_lo(LB + B_FF + n + 2, s)
                    v.wait_ge(sq_v, l * 32 + 8 * c + m + 1)
                    v.wait_ge(ghi_made, l * 32 + 8 * c + m + 1)
                    v.tensor_tensor(lo, ts[:, :], f32(hi), ALU.subtract).then_inc(hid_made, 1)

                inverse(S_SUM2, l * NS, l * 6 + 3)
                for m in range(KD):
                    hidden(m, 0, m, m % 2, ghi[:, m, :], glo[:, m, :])
                with v.Fori(0, FFC - 1) as c:
                    with v.Fori(0, KD // 2) as m2:
                        for odd in range(2):
                            n = 16 * c + 8 + 2 * m2 + odd
                            add_to_x(T_FF + n, 2 * m2 + odd, odd)
                            split_lo(LB + B_FF + n + 2, odd)
                    with v.Fori(0, KD // 2) as m2:
                        for odd in range(2):
                            m = 2 * m2 + odd
                            hidden(16 * c + 16 + m, c + 1, m, odd, tile_of(ghi, m), tile_of(glo, m))
                for m in range(KD):
                    n = 16 * (FFC - 1) + 8 + m
                    add_to_x(T_FF + n, m, m % 2)
                    split_lo(LB + B_FF + n + 2, m % 2)
                    low_h(m, l * 16 + 16 + m, lp[:, L_NEXT:L_NEXT + KD])
                step.leave(LAYERS, DVE_STEPS)

            inverse(S_SUM1, LAYERS * NS, LAYERS * 6)
            v.wait_ge(x_kept, 16 * KD * (LAYERS + 1))
            for m in range(KD):
                v.scalar_tensor_tensor(x[:, m, :], x[:, m, :], lp[:, L_NEXT + m:L_NEXT + m + 1], rms[:, :],
                                       ALU.mult, ALU.mult).then_inc(y_made, 1)

        @block.gpsimd
        def _(pool):
            step = Steps(pool, pool_s)

            def add_squares(phase_no):
                for m in range(1, KD):
                    if isinstance(phase_no, int):
                        pool.wait_ge(sq_made, 1)
                        pool.wait_ge(*((first_sq, (m + 1) // 2) if m % 2 else (sq_made, m // 2 + 1)))
                    else:
                        pool.wait_ge(sq_made, 8 * phase_no - 4 + m + 1)
                    if m > 1:
                        pool.wait_ge(sq_added, 7 * phase_no + m - 1)
                    pool.tensor_tensor(rms[:, :], rms[:, :], (tr, ts)[m % 2][:, :], ALU.add).then_inc(sq_added, 1)

            pool.wait_ge(zero_set, 1)
            pool.dma_start(k_dram[:, :, 0:112], zero[:, :].unsqueeze(1).broadcast_to([CH, GROUPS, 112])).then_inc(k_zero, 16)
            pool.wait_ge(k_zero, 16)
            add_squares(0)

            with pool.Fori(0, LAYERS) as l:
                step.enter(l, POOL_STEPS)

                def tt(out, a, b, op):
                    step(pool.tensor_tensor(out, a, b, op))

                def of(dram):
                    return dram[bass.ds(l, 1)].rearrange("a p n -> (a p) n")

                pool.wait_ge(tile_free, l * NT + 2)
                pool.wait_ge(h_made, l * 16 + 8)
                pool.sem_inc(pool_passed, 1)
                pool.dma_start(pp[:, :], of(prep_in)).then_inc(pp_in, 16)
                pool.dma_start(lp[:, :], of(layer_in)).then_inc(lp_in, 16)
                pool.wait_ge(x_kept, 16 * KD * (l + 1))
                pool.sem_inc(pool_passed, 1)
                pool.dma_start(wp[:, :, :].rearrange("p k d -> p (k d)"), of(w_pool)).then_inc(wp_in, 16)

                def carry_weights(q):
                    if q:
                        pool.wait_ge(small_done, l * NS + S_PREP + 8 * q - 4)
                        pool.wait_ge(cy_out, 32 * (l * 4 + q))
                    cr = pp[:, C_CRE:C_CRE + 256].rearrange("p (g c) -> p g c", c=CH)
                    ci = pp[:, C_CIM:C_CIM + 256].rearrange("p (g c) -> p g c", c=CH)
                    pr, pi = (t[:, BLK:2 * BLK + 1, 4 * q:4 * q + 4].rearrange("p m g -> p g m").unsqueeze(3)
                              .broadcast_to([P, 4, BLK + 1, CH]) for t in (pwr, pwi))
                    t0, t1 = (pt[:, i, :].rearrange("p (g m c) -> p g m c", m=BLK + 1, c=CH) for i in range(2))
                    for ri, ab in enumerate(((cr, ci), (nci, cr))):
                        a, b = (t[:, 4 * q:4 * q + 4, :].unsqueeze(2).broadcast_to([P, 4, BLK + 1, CH]) for t in ab)
                        step.wait()
                        tt(t0, pr, a, ALU.mult)
                        tt(t1, pi, b, ALU.mult)
                        step.wait()
                        if ri == 0:
                            tt(yq[:, ri, :, :, :], t0, t1, ALU.subtract)
                    pool.tensor_tensor(yq[:, 1, :, :, :], t0, t1, ALU.subtract).then_inc(y_quart, 1)
                    pool.wait_ge(y_quart, l * 4 + q + 1)

                def rotations(h, rot, tmp, th):
                    pool.sem_inc(pool_passed, 1)
                    for i in range(2):
                        step(pool.tensor_copy(rot[:, i, :, 0:1], th[:, i, :].unsqueeze(2)))
                    n = 1
                    while n < JP:
                        double(step, pool.tensor_tensor, pool.tensor_copy, tmp, rot, n, rot_made)
                        n *= 2
                    pool.wait_ge(rot_made, l * 2 + h + 1)

                pool.wait_ge(prep_v, l * 2 + 2)
                carry_weights(0)
                rotations(0, rot01[:, :, 4:8, :], pt, phase[:, :, 4:8])
                for q in range(1, 4):
                    carry_weights(q)
                pool.wait_ge(tile_done, l * NT + KD)
                rotations(1, rot23[:, :, 4:8, :], ptmp, phase[:, :, 12:16])
                pool.wait_ge(dd_in, 16 * (l + 1))
                q = 3
                pool.wait_ge(small_free, l * NS + S_PREP + 8 * q + 8 + 2)
                rotate(step, pool.tensor_tensor, ptmp, q, w, zh, 0, -1, pre_p)
                pool.wait_ge(pre_p, l + 1)
                for n, q in enumerate((0, 3)):
                    pool.wait_ge(scan_v, l * 4 + (1, 3)[n])
                    rotate(step, pool.tensor_tensor, ptmp, q, w, zh, 1, 1)
                    step.wait()
                    pool.sem_inc(pool_passed, 1)
                    pool.memset(quarter(zh, q, slice(None), slice(0, 1)), 0.0)
                    for ri in range(2):
                        ins = pool.tensor_copy(quarter(zh, q, ri, slice(JP, JP + 1)),
                                               dd[:, D_INIT + ri * GP + 4 * q:D_INIT + ri * GP + 4 * q + 4].unsqueeze(2))
                    ins.then_inc(st_p, 1)
                    pool.wait_ge(st_p, l * 2 + n + 1)
                pool.wait_ge(scan_v, l * 4 + 4)
                pool.wait_ge(st_v, l * 2 + 2)
                n = 0
                for s, (i, j) in enumerate(((JP - 1, JP - 1), (JS - 1, J - 1))):
                    for h, rot in enumerate((rot01, rot23)):
                        g = slice(8 * h, 8 * h + 8)
                        cos, sin = (rot[:, r, :, i:i + 1] for r in range(2))
                        re, im = (w[:, g, r, j:j + 1] for r in range(2))
                        t0, t1 = (ptmp[:, r, 0:8].unsqueeze(2) for r in range(2))
                        for ri, (u, w_, op) in enumerate(((re, im, ALU.subtract), (im, re, ALU.add))):
                            if n:
                                pool.wait_ge(fin_made, 8 * l + n)
                            tt(t0, cos, u, ALU.mult)
                            tt(t1, sin, w_, ALU.mult)
                            step.wait()
                            pool.tensor_tensor(fin[:, s, ri, g].unsqueeze(2), t0, t1, op).then_inc(fin_made, 1)
                            n += 1
                pool.wait_ge(fin_made, 8 * (l + 1))
                pool.sem_inc(pool_passed, 1)
                pool.dma_start(of(ssm_out), fin[:, :, :, :].rearrange("p s r g -> p (s r g)")).then_inc(fin_out, 16)
                add_squares(2 * l + 1)
                add_squares(2 * l + 2)
                step.leave(LAYERS, POOL_STEPS)


DVE_STEPS = 216
POOL_STEPS = 141


def _frames(xp, xs):
    d = xp.shape[-1]
    a = np.concatenate([xp.reshape(JP, BLK, d), xs.reshape(JS, BLK, d)], axis=0)
    return np.ascontiguousarray(a.transpose(2, 1, 0)).reshape(d // P, P, T)


def _lhs(wt, k0, n_k, m):
    return wt[k0 * P:(k0 + n_k) * P, m * P:(m + 1) * P].reshape(n_k, P, P).transpose(1, 0, 2).reshape(P, n_k * P)


def _pairs(a):
    return np.moveaxis(a.reshape(GP, 2, ST, *a.shape[2:]), 0, 2).reshape(P, GP, *a.shape[2:])


def kernel(**inputs):
    import concourse.bacc as bacc
    from concourse.bass_utils import run_bass_kernel_spmd as run

    a = {k: np.asarray(v) for k, v in inputs.items()}
    f = np.float32
    x_in = _frames(a["x_prompt"][0], a["x_sample"][0])
    blocks = []
    for l in range(LAYERS):
        w_in, w_out, w_glu = a["w_in"][l], a["w_out"][l], a["w_glu"][l]
        blocks += [_lhs(w_in, 0, KD, m) for m in (0, 1, 2, 3, 7, 6, 5, 4)]
        for wt, k0, n in ((w_out, KA, KD), (w_glu, 0, KA), (w_out, 0, KD)):
            blocks += [np.concatenate([_lhs(wt, k0, KA, m), _lhs(wt, k0, KA, m + 1)], 1) for m in range(0, n, 2)]
        for c in range(FFC):
            blocks += [_lhs(a["w_ff1"][l], 0, KD, KD * c + m) for m in range(KD)]
            blocks += [_lhs(a["w_ff2"][l], KD * c, KD, m) for m in range(KD)]
    blocks += blocks[:2]
    w_blocks = np.stack(blocks)
    w_pool = np.ascontiguousarray(a["w_pool"].transpose(0, 2, 1, 3)).reshape(LAYERS, P, KA * P)

    prep = np.zeros((LAYERS, P, NPP), f)
    ms = np.array([*range(BLK - 1, -1, -1), *range(BLK + 1)], f)
    prep[:, :, C_M:C_M + NM * GP] = np.repeat(ms, GP)
    prep[:, :, C_ID:C_ID + P] = np.eye(P, dtype=f)
    t = np.arange(2 * BLK).reshape(2, BLK).T
    for k in range(KA):
        win = 2 << k
        prep[:, :, C_RC + 16 * k:C_RC + 16 * k + 16] = (win / np.minimum(t + 1, win)).astype(f).reshape(-1)
    layer = np.zeros((LAYERS, P, NLP), f)
    dstate = np.zeros((LAYERS, P, ND), f)
    col = lambda g: g.reshape(-1, P).T
    for l in range(LAYERS):
        prep[l, :, C_LRE:C_LRE + GP] = _pairs(a["ssm_lambda_re"][l])
        prep[l, :, C_LIM:C_LIM + GP] = _pairs(a["ssm_lambda_im"][l])
        prep[l, :, C_LDT:C_LDT + GP] = _pairs(np.repeat(a["ssm_log_dt"][l][:, None], ST, 1))
        for o, name in ((C_BRE, "ssm_b_re"), (C_BIM, "ssm_b_im")):
            prep[l, :, o:o + 256] = _pairs(a[name][l]).reshape(P, 256)
        for o, name in ((C_CRE, "ssm_c_re"), (C_CIM, "ssm_c_im")):
            prep[l, :, o:o + 256] = _pairs(a[name][l].transpose(0, 2, 1)).reshape(P, 256)
        h = np.concatenate([np.zeros((1, KA * P), f), a["state_pool"][l, 0]], 0)
        prep[l, :, C_HIST:C_HIST + 64] = h.reshape(2, BLK, KA, P).transpose(3, 2, 1, 0).reshape(P, 64)
        layer[l, :, L_FFN:L_FFN + KD] = col(a["g_ffn"][l])
        layer[l, :, L_NEXT:L_NEXT + KD] = col(a["g_mix"][l + 1] if l + 1 < LAYERS else a["g_final"])
        layer[l, :, L_SCALE:L_SCALE + KA] = col(a["pool_scale"][l])
        d = a["ssm_d"][l].reshape(GROUPS, CH).T
        dstate[l, :, D_D:D_D + GROUPS] = np.tile(d, (BLK, 1))
        dstate[l, :, D_INIT:D_INIT + GP] = _pairs(a["state_ssm_re"][l, 0])
        dstate[l, :, D_INIT + GP:D_INIT + 2 * GP] = _pairs(a["state_ssm_im"][l, 0])
    gain0 = np.ascontiguousarray(col(a["g_mix"][0]))

    nc = bacc.Bacc("TRN2", target_bir_lowering=False, num_devices=1)
    arrays = {"x_t": x_in, "w_blocks": w_blocks, "w_pool_t": w_pool, "prep": prep, "gain0": gain0,
              "layer": layer, "dstate": dstate}
    args = [nc.dram_tensor(n, v.shape, F32, kind="ExternalInput").ap() for n, v in arrays.items()]
    outs = {"y_t": (KD, P, T), "pool_t": (LAYERS, P, 128), "ssm_t": (LAYERS, P, 64)}
    args += [nc.dram_tensor(n, s, F32, kind="ExternalOutput").ap() for n, s in outs.items()]
    hybrid_trunk(nc, *args)
    r = run(nc, [arrays], core_ids=[0]).results[0]

    y = r["y_t"].reshape(DM, BLK, J).transpose(2, 1, 0)
    y_prompt = np.ascontiguousarray(y[:JP]).reshape(1, SEQ, DM)
    y_sample = np.ascontiguousarray(y[JP:]).reshape(1, DSEQ, DM)
    h = r["pool_t"].reshape(LAYERS, P, KA, BLK, 2, 2).transpose(4, 0, 5, 3, 2, 1).reshape(2, LAYERS, 1, 2 * BLK, KA * P)
    h = np.ascontiguousarray(h[:, :, :, 1:])
    s = r["ssm_t"].reshape(LAYERS, 2, ST, 2, 2, GP).transpose(3, 4, 0, 5, 1, 2).reshape(2, 2, LAYERS, 1, GROUPS, ST)
    s = np.ascontiguousarray(s)
    return (y_prompt, y_sample, s[0, 0], s[0, 1], h[0], s[1, 0], s[1, 1], h[1])
```
